# Optimizing a Trainium2 kernel written in Bass

```python
import jax, jax.numpy as jnp
from jax import lax
import numpy as np

D_MODEL = 2048
BATCH = 1
SEQ = 256
DEPTH = 1

CHUNK = 64
EPS = 1e-6
RET_HEADS = 8
RET_QK_DIM = D_MODEL // 16
RET_V_DIM = D_MODEL // 8
RET_QK_WIDTH = RET_HEADS * RET_QK_DIM
RET_V_WIDTH = RET_HEADS * RET_V_DIM
ROPE_BASE = 10000.0
ATT_HEAD_DIM = 64
ATT_Q_HEADS = D_MODEL // ATT_HEAD_DIM
ATT_KV_HEADS = ATT_Q_HEADS // 8
ATT_Q_WIDTH = ATT_Q_HEADS * ATT_HEAD_DIM
ATT_KV_WIDTH = ATT_KV_HEADS * ATT_HEAD_DIM
ATT_WINDOW = 128
WIN_CHUNKS = ATT_WINDOW // CHUNK
SPLITS = (RET_QK_WIDTH, RET_QK_WIDTH, RET_V_WIDTH, RET_V_WIDTH, ATT_Q_WIDTH, ATT_KV_WIDTH, ATT_KV_WIDTH)
IN_WIDTH = sum(SPLITS)
N_BRANCHES = 2
D_FF = 4 * D_MODEL

kernel_name = "hybrid_retention_swa_sink_gated_block"

def rms_norm(x, g):
    xf = x.astype(jnp.float32)
    y = xf * lax.rsqrt(jnp.mean(xf * xf, axis=-1, keepdims=True) + EPS)
    return (y * g.astype(jnp.float32)).astype(x.dtype)

def rotary(t, pos):
    half = t.shape[-1] // 2
    inv = ROPE_BASE ** (-jnp.arange(half, dtype=jnp.float32) / half)
    ang = pos[:, None] * inv[None, :]
    cos = jnp.cos(ang)[None, :, None, :]
    sin = jnp.sin(ang)[None, :, None, :]
    tf = t.astype(jnp.float32)
    t1, t2 = tf[..., :half], tf[..., half:]
    return jnp.concatenate([t1 * cos - t2 * sin, t1 * sin + t2 * cos], axis=-1)

def retention_chunkwise(q, k, v):
    b, s, h, dk = q.shape
    dv = v.shape[-1]
    nc = s // CHUNK
    log_gamma = jnp.log1p(-jnp.exp2(-5.0 - jnp.arange(h, dtype=jnp.float32)))
    qc = q.astype(jnp.float32).reshape(b, nc, CHUNK, h, dk)
    kc = (k.astype(jnp.float32) * dk ** -0.5).reshape(b, nc, CHUNK, h, dk)
    vc = v.astype(jnp.float32).reshape(b, nc, CHUNK, h, dv)
    pos = jnp.arange(CHUNK, dtype=jnp.float32)
    intra_decay = jnp.exp(log_gamma[:, None, None] * jnp.abs(pos[:, None] - pos[None, :]))
    scores = jnp.einsum('bnihd,bnjhd->bnhij', qc, kc) * intra_decay
    intra = jnp.einsum('bnhij,bnjhe->bnihe', scores, vc)
    k_decay = jnp.exp(log_gamma[:, None] * (CHUNK - 1 - pos)[None, :])
    kv = jnp.einsum('bnjhd,hj,bnjhe->nbhde', kc, k_decay, vc)
    chunk_decay = jnp.exp(log_gamma * CHUNK)[:, None, None]

    def step(state, kv_n):
        return state * chunk_decay + kv_n, state

    init = jnp.zeros((b, h, dk, dv), jnp.float32)
    _, states = lax.scan(step, init, kv)
    q_decay = jnp.exp(log_gamma[:, None] * (pos + 1.0)[None, :])
    inter = jnp.einsum('bnihd,hi,nbhde->bnihe', qc, q_decay, states)
    return (intra + inter).reshape(b, s, h, dv)

def sliding_window_gqa_sinks(q, k, v, sinks):
    b, s, hq, dh = q.shape
    hkv = k.shape[2]
    g = hq // hkv
    nc = s // CHUNK
    prev = WIN_CHUNKS - 1
    qc = q.reshape(b, nc, CHUNK, hkv, g, dh)

    def windows(t):
        tp = jnp.pad(t.reshape(b, nc, CHUNK, hkv, dh), ((0, 0), (prev, 0), (0, 0), (0, 0), (0, 0)))
        return jnp.concatenate([tp[:, i:i + nc] for i in range(WIN_CHUNKS)], axis=2)

    kw, vw = windows(k), windows(v)
    logits = jnp.einsum('bnqhgd,bnkhd->bhgnqk', qc, kw).astype(jnp.float32) * (dh ** -0.5)
    key_chunk = jnp.arange(nc)[:, None] - prev + jnp.arange(WIN_CHUNKS * CHUNK)[None, :] // CHUNK
    valid = (key_chunk >= 0)[:, None, :]
    logits = jnp.where(valid, logits, -jnp.inf)
    sink = sinks.astype(jnp.float32).reshape(hkv, g)[None, :, :, None, None, None]
    m = jnp.maximum(jnp.max(logits, axis=-1, keepdims=True), sink)
    p = jnp.exp(logits - m)
    p = p / (jnp.sum(p, axis=-1, keepdims=True) + jnp.exp(sink - m))
    out = jnp.einsum('bhgnqk,bnkhd->bnqhgd', p.astype(v.dtype), vw)
    return out.reshape(b, s, hq * dh)

def setup_inputs(seed: int = 0) -> dict:
    key = jax.random.key(seed)
    ks = jax.random.split(key, 14)
    f32 = jnp.float32

    def w(k, shape, fan_in):
        return jax.random.normal(k, shape, f32) * (fan_in ** -0.5)

    def gain(k, shape):
        return 1.0 + 0.02 * jax.random.normal(k, shape, f32)

    return {
        "x": jax.random.normal(ks[0], (BATCH, SEQ, D_MODEL), f32),
        "norm_mix_g": gain(ks[1], (DEPTH, D_MODEL)),
        "w_in": w(ks[2], (DEPTH, D_MODEL, IN_WIDTH), D_MODEL),
        "ret_norm_g": gain(ks[3], (DEPTH, RET_V_WIDTH)),
        "attn_sinks": 0.5 * jax.random.normal(ks[4], (DEPTH, ATT_Q_HEADS), f32),
        "w_ret_branch": w(ks[5], (DEPTH, RET_V_WIDTH, D_MODEL), RET_V_WIDTH),
        "w_attn_branch": w(ks[6], (DEPTH, ATT_Q_WIDTH, D_MODEL), ATT_Q_WIDTH),
        "w_gate": w(ks[7], (DEPTH, D_MODEL, N_BRANCHES * D_MODEL), D_MODEL),
        "w_out": w(ks[8], (DEPTH, D_MODEL, D_MODEL), D_MODEL),
        "norm_ffn_g": gain(ks[9], (DEPTH, D_MODEL)),
        "w_up": w(ks[10], (DEPTH, D_MODEL, D_FF), D_MODEL),
        "w_down": w(ks[11], (DEPTH, D_FF, D_MODEL), D_FF),
        "norm_final_g": gain(ks[12], (D_MODEL,)),
    }

def reference(x, norm_mix_g, w_in, ret_norm_g, attn_sinks, w_ret_branch, w_attn_branch,
              w_gate, w_out, norm_ffn_g, w_up, w_down, norm_final_g):
    b, s, _ = x.shape
    pos = jnp.arange(s, dtype=jnp.float32)
    offsets = np.cumsum(SPLITS)[:-1].tolist()
    for l in range(DEPTH):
        h = rms_norm(x, norm_mix_g[l])
        proj = jnp.einsum('bsd,de->bse', h, w_in[l])
        rq, rk, rv, rg, aq, ak, av = jnp.split(proj, offsets, axis=-1)
        rq = rotary(rq.reshape(b, s, RET_HEADS, RET_QK_DIM), pos)
        rk = rotary(rk.reshape(b, s, RET_HEADS, RET_QK_DIM), pos)
        ret = retention_chunkwise(rq, rk, rv.reshape(b, s, RET_HEADS, RET_V_DIM))
        ret = ret * lax.rsqrt(jnp.mean(ret * ret, axis=-1, keepdims=True) + EPS)
        ret = ret.reshape(b, s, RET_V_WIDTH) * ret_norm_g[l].astype(jnp.float32)
        ret = (jax.nn.silu(rg.astype(jnp.float32)) * ret).astype(x.dtype)
        y_ret = jnp.einsum('bse,ed->bsd', ret, w_ret_branch[l])
        att = sliding_window_gqa_sinks(aq.reshape(b, s, ATT_Q_HEADS, ATT_HEAD_DIM),
                                       ak.reshape(b, s, ATT_KV_HEADS, ATT_HEAD_DIM),
                                       av.reshape(b, s, ATT_KV_HEADS, ATT_HEAD_DIM),
                                       attn_sinks[l])
        y_att = jnp.einsum('bse,ed->bsd', att, w_attn_branch[l])
        gates = jax.nn.sigmoid(jnp.einsum('bsd,de->bse', h, w_gate[l]).astype(jnp.float32))
        g_ret, g_att = jnp.split(gates, N_BRANCHES, axis=-1)
        merged = (g_ret * y_ret.astype(jnp.float32) + g_att * y_att.astype(jnp.float32)).astype(x.dtype)
        x = x + jnp.einsum('bsd,de->bse', merged, w_out[l])
        h2 = rms_norm(x, norm_ffn_g[l])
        u = jnp.square(jax.nn.relu(jnp.einsum('bsd,df->bsf', h2, w_up[l])))
        x = x + jnp.einsum('bsf,fd->bsd', u, w_down[l])
    return rms_norm(x, norm_final_g)


_drawn_inputs = setup_inputs


def setup_inputs(seed=0):
    import zlib

    import numpy as np

    out = dict(_drawn_inputs(seed))
    spreads = {}
    factors = {'norm_mix_g': 3.837,
     'ret_norm_g': 22.49,
     'attn_sinks': 195.07,
     'norm_ffn_g': 11.478,
     'norm_final_g': 24.535}
    for name, (base, spread) in spreads.items():
        noise = np.random.default_rng([zlib.crc32(name.encode()), seed]).standard_normal(out[name].shape)
        drawn = base * np.exp(spread * noise) if base else spread * noise
        out[name] = __import__('jax').numpy.asarray(drawn.astype(out[name].dtype))
    for name, factor in factors.items():
        out[name] = (out[name] * factor).astype(out[name].dtype)
    return out
```

```python
import concourse.bass as bass
from concourse import mybir
from contextlib import ExitStack
import numpy as np

P = 128
D = 2048
S = 256
TILES = S // P
COLS = 512
KCH = D // P
UNITS = 8
UCH = KCH // UNITS
LOADS = 4
GROUPS = D // COLS
GCH = COLS // P
EPS = 1e-6
CHUNK = 64
NCHUNK = S // CHUNK
RET_HEADS = 8
RET_QK = D // 16
RET_V = D // 8
ATT_D = 64
KV_HEADS = 4
RET_COLS = S + (S - P)
ATT_SCALE = ATT_D ** -0.5
OFF_RQK = 0
OFF_RV = 2 * RET_HEADS * RET_QK
OFF_RG = OFF_RV + D
OFF_AQ = OFF_RG + D
OFF_AKV = OFF_AQ + D
SMALL = P + 2 * TILES * (RET_QK // 2) + 4 * KCH
KEYS = [(0, CHUNK, 0), (0, 2 * CHUNK, 0), (CHUNK, 2 * CHUNK, 1), (2 * CHUNK, 2 * CHUNK, 2)]


class Block:

    def __init__(self, first, step=0, j=0):
        self.number = j * step + first
        self.parity = first % 2
        self.turn = j * (step // 2) + first // 2
        self.reused = first >= 2
        self.very_first = first == 0

    def unit(self, u):
        return self.number * UNITS + (u + 1)


def later(n):
    return not (type(n) is int and n == 0)


class Steps:

    def __init__(self, sem):
        self.sem, self.base, self.here, self.total = sem, 0, 0, 0

    def step(self, instruction):
        instruction.then_inc(self.sem, 1)
        self.here += 1
        self.total += 1

    def wait(self, engine):
        engine.wait_ge(self.sem, self.base + self.here)

    def enter_loop(self, j, first, per):
        self.before, self.base, self.here = self.total, j * per + (self.total - first * per), 0

    def leave_loop(self, turns, per):
        assert self.here == per, (self.here, per)
        self.total = self.before + turns * per
        self.base, self.here = self.total, 0


OWN_STAGE1, OWN_STAGE2, OWN_STAGE3, OWN_STAGE4 = 18, 1, 1, 1


def build(nc, x, w_in, w_ret, w_att, w_gate, w_out, w_up, w_down, g_fin,
          small_c, decay_c, out):
    f32, f32r = mybir.dt.float32, mybir.dt.float32r
    ALU, ACT, AX = mybir.AluOpType, mybir.ActivationFunctionType, mybir.AxisListType
    ds = bass.ds

    ctx = ExitStack()
    with ctx:
        here = [(nc.sbuf_base + 63) // 64 * 64]

        def place(name, shape, dt, at=None):
            size = int(np.prod(shape[1:])) * 4
            if at is None:
                at = here[0]
                here[0] += (size + 31) // 32 * 32
            return nc.alloc_sbuf_tensor_at(name, shape, dt, offset=at)

        def sem(name):
            return ctx.enter_context(nc.semaphore(name))

        K = 1024
        at_a = here[0]
        ta_hi = place("ta_hi", [P, KCH, S], f32r)
        ta_lo = place("ta_lo", [P, KCH, S], f32r)
        at_b = here[0]
        tb_hi = place("tb_hi", [P, KCH, S], f32r)
        tb_lo = place("tb_lo", [P, KCH, S], f32r)
        at_c = here[0]
        tc_hi = place("tc_hi", [P, KCH, S], f32r)
        tc_lo = place("tc_lo", [P, KCH, S], f32r)
        at_m = here[0]
        mix = place("mix", [P, TILES, D], f32)
        raw = place("raw", [P, KCH, COLS], f32)
        whi = place("whi", [P, KCH // 2, COLS], f32r)
        wlo = place("wlo", [P, KCH // 2, COLS], f32r)
        buf = [place(f"buf{i}", [P, TILES, COLS], f32) for i in range(4)]
        gfin = place("gfin", [P, D], f32)
        kst = place("kst", [P, 2, S], f32)
        vst = place("vst", [P, 3, P], f32)
        half_qk = RET_QK // 2
        small = place("small", [P, SMALL], f32)
        ident = small[:, 0:P]
        rope = small[:, P:P + 2 * TILES * half_qk].rearrange("p (a t d) -> p a t d", a=2, t=TILES)
        gmix, gret, gffn, sink = [small[:, SMALL - (4 - i) * KCH:SMALL - (3 - i) * KCH] for i in range(4)]
        roper = place("roper", [P, 2, TILES, half_qk], f32)
        nsink = place("nsink", [P, 16], f32)
        ssq = place("ssq", [P, 2], f32)
        msq = place("msq", [P, 4], f32)
        rstd = place("rstd", [P, 2], f32)
        rstd_half = place("rstd_half", [P, 2], f32)
        ssq2 = place("ssq2", [P, TILES, GROUPS], f32)
        sum2 = place("sum2", [P, 2], f32)
        rstd2 = place("rstd2", [P, 2], f32)
        rstd3 = place("rstd3", [P, 2], f32)
        ssqr = place("ssqr", [P, 2, TILES], f32)
        powr = place("powr", [P, 2, TILES], f32)
        retsc = place("retsc", [P, 2, TILES], f32)
        mhalf = place("mhalf", [P, 4], f32)
        mx = place("mx", [P, 4], f32)
        negm = place("negm", [P, 4], f32)
        esd = place("esd", [P, 4], f32)
        es = place("es", [P, 4], f32)
        sums = place("sums", [P, 4], f32)
        den = place("den", [P, 4], f32)
        rden = place("rden", [P, 4], f32)
        assert here[0] <= nc.sbuf_usable_end, here[0]
        xin = place("xin", [P, TILES, D], f32, at_b)
        junk = place("junk", [P, D], f32, at_c + 24 * K)
        qkT = place("qkT", [P, 2 * RET_HEADS, S], f32, at_c)
        qbd = place("qbd", [P, 4, NCHUNK, P], f32, at_c + 16 * K)
        decay = place("decay", [P, RET_HEADS, RET_COLS], f32, at_c + 16 * K)
        ptr = place("ptr", [P, 2, RET_COLS], f32, at_c + 28 * K)
        final = place("final", [P, TILES, D], f32, at_c)
        kT = place("kT", [P, KV_HEADS, S], f32, at_m)
        vwin = place("vwin", [P, 3, KV_HEADS, P], f32, at_m + 4 * K)
        prob = place("prob", [P, 4, P], f32, at_m + 10 * K)
        probT = place("probT", [P, 4, P], f32, at_m + 12 * K)

        acc = [ctx.enter_context(nc.psum_tensor(f"acc{i}", [P, TILES, COLS], f32)) for i in range(2)]
        tps = ctx.enter_context(nc.psum_tensor("tps", [P, GCH, S], f32))
        sps = ctx.enter_context(nc.psum_tensor("sps", [P, 4, P], f32))
        pps = ctx.enter_context(nc.psum_tensor("pps", [P, 4, P], f32))
        flat = "p a b -> p (a b)"
        rs_ps = [sps[:].rearrange(flat), pps[:].rearrange(flat)]
        out_ps = tps[:].rearrange("p (i t) e -> p i t e", t=TILES)

        raw_full = [sem(f"raw_full{s}") for s in range(LOADS)]
        hi_ready, lo_ready, unit_done = sem("hi_ready"), sem("lo_ready"), sem("unit_done")
        evacuated = [sem("evacuated0"), sem("evacuated1")]
        x_full = [sem(f"x_full{g}") for g in range(GROUPS)]
        const_full, fin_full = sem("const_full"), sem("fin_full")
        decay_full = sem("decay_full")
        xres_full = [sem(f"xres_full{j}") for j in range(GROUPS)]
        t_full, t_free = sem("t_full"), sem("t_free")
        t_hi = sem("t_hi")
        hT_ready, retT_ready, h2T_ready = sem("hT_ready"), sem("retT_ready"), sem("h2T_ready")
        own = sem("own")
        mhalf_set, ssq_ready, ms_ready = sem("mhalf_set"), sem("ssq_ready"), sem("ms_ready")
        pow_ready, rstd_ready = sem("pow_ready"), sem("rstd_ready")
        consts_ready = sem("consts_ready")
        vshift, vst_ready, rope_ready = sem("vshift"), sem("vst_ready"), sem("rope_ready")
        s_full, negm_ready, exp_done, p_ready = sem("s_full"), sem("negm_ready"), sem("exp_done"), sem("p_ready")
        pt_full, pt_ready, av_full, att_hi, att_lo = sem("pt_full"), sem("pt_ready"), sem("av_full"), sem("att_hi"), sem("att_lo")
        kst_ready, rs_full, ptr_ready = sem("kst_ready"), sem("rs_full"), sem("ptr_ready")
        rssq_ready, rms_ready, rpow_ready, ret_ready = sem("rssq_ready"), sem("rms_ready"), sem("rpow_ready"), sem("ret_ready")
        rgate_ready, gated_ready = sem("rgate_ready"), sem("gated_ready")
        m_ready, u_ready = sem("m_ready"), sem("u_ready")
        x1_sq, ms2_ready, rstd2_ready = sem("x1_sq"), sem("ms2_ready"), sem("rstd2_ready")
        down_sq, ms3_ready, rstd3_ready = sem("down_sq"), sem("ms3_ready"), sem("rstd3_ready")
        final_g, final_act, final_dve, stored = sem("final_g"), sem("final_act"), sem("final_dve"), sem("stored")

        T_X, T_K = 0, GROUPS
        T_STAGE1 = T_K + 1
        T_STAGE3 = T_STAGE1 + 8
        T_STAGE4 = T_STAGE3 + 8
        T_STAGE5 = T_STAGE4 + 4
        T_STAGE6 = T_STAGE5 + 4
        B1, B2, B3, B4, B5, B6 = 1, 9, 17, 25, 33, 37

        block = ctx.enter_context(nc.Block())

        @block.sync
        def _(sp):
            def load(B, src, s):
                src = src.rearrange("(k p) n -> p k n", p=P)
                sp.lower_ap_dma(src)
                if not B.very_first:
                    sp.wait_ge(lo_ready, B.number * UNITS + (2 * s + 2 - UNITS))
                sp.dma_start(raw[:, GCH * s:GCH * (s + 1), :],
                             src).then_inc(raw_full[s], 16)

            def load_block(B, w, col, row=0):
                for s in range(LOADS):
                    load(B, w[ds(row + s * 512, 512), ds(col, COLS)], s)

            for g in range(GROUPS):
                cols = slice(g * COLS, (g + 1) * COLS)
                sp.dma_start(xin[:, :, cols], x[:, cols].rearrange("(t p) n -> p t n", p=P)).then_inc(x_full[g], 16)
            load_block(Block(0), w_in, OFF_AKV)

            def stage1(j):
                load_block(Block(B1, 2, j), w_in, j * COLS + OFF_AQ)
                load_block(Block(B1 + 1, 2, j), w_in, j * COLS + OFF_RQK)

            def stage2(j):
                load_block(Block(B2, 2, j), w_gate, j * COLS + D)
                load_block(Block(B2 + 1, 2, j), w_att, j * COLS)

            def stage3(j):
                load_block(Block(B3, 2, j), w_in, j * COLS + OFF_RV)
                load_block(Block(B3 + 1, 2, j), w_in, j * COLS + OFF_RG)

            def stage4(j):
                load_block(Block(B4, 2, j), w_gate, j * COLS)
                load_block(Block(B4 + 1, 2, j), w_ret, j * COLS)

            stage1(0)
            with sp.Fori(1, 4) as j:
                stage1(j)
            stage2(0)
            with sp.Fori(1, 4) as j:
                stage2(j)
            sp.wait_ge(s_full, 16)
            sp.dma_start(decay[:], decay_c).then_inc(decay_full, 16)
            stage3(0)
            with sp.Fori(1, 4) as j:
                stage3(j)
            sp.dma_start(gfin[:], g_fin.partition_broadcast(P)).then_inc(fin_full, 16)
            stage4(0)
            with sp.Fori(1, 4) as j:
                stage4(j)
            for j in range(GROUPS):
                if j == GROUPS - 1:
                    load_block(Block(B5), w_out, 0)
                sp.wait_ge(m_ready, j + 1)
                sp.dma_start(mix[:, :, j * COLS:(j + 1) * COLS],
                             x[:, j * COLS:(j + 1) * COLS].rearrange("(t p) n -> p t n", p=P)).then_inc(xres_full[j], 16)
            for j in range(1, GROUPS):
                load_block(Block(B5 + j), w_out, j * COLS)

            def stage6(q):
                for i in range(4):
                    load_block(Block(B6 + i, 8, q), w_up, q * D + i * COLS)
                for i in range(4):
                    load_block(Block(B6 + 4 + i, 8, q), w_down, i * COLS, q * D)

            stage6(0)
            with sp.Fori(1, 4) as q:
                stage6(q)
            for t, ready in ((0, final_act), (1, final_dve)):
                for h in range(2):
                    sp.wait_ge(ready, h + 1)
                    sp.dma_start(out[t * P:(t + 1) * P, h * 1024:(h + 1) * 1024],
                                 final[:, t, h * 1024:(h + 1) * 1024]).then_inc(stored, 16)
            sp.wait_ge(stored, 64)

        @block.tensor
        def _(pe):
            def gemm(B, hi, lo, u0, u1):
                for u in range(u0, u1):
                    if u == 0 and B.reused:
                        pe.wait_ge(evacuated[B.parity], B.turn)
                    pe.wait_ge(lo_ready, B.unit(u))
                    for kk in range(UCH):
                        k, slot = u * UCH + kk, (u * UCH + kk) % (KCH // 2)
                        for t in range(TILES):
                            tok = slice(t * P, (t + 1) * P)
                            for n, (a, b) in enumerate(((hi, whi), (hi, wlo), (lo, whi))):
                                last = nc.tensor.matmul(acc[B.parity][:, t, :], a[:, k, tok], b[:, slot, :],
                                                        start=(k == 0 and n == 0), stop=(k == KCH - 1 and n == 2))
                    last.then_inc(unit_done, 1)

            def transposes(turn, src):
                if later(turn):
                    pe.wait_ge(t_free, turn)
                for m in range(GCH):
                    for t in range(TILES):
                        last = nc.tensor.transpose(tps[:, m, t * P:(t + 1) * P], src(t, m), ident)
                last.then_inc(t_full, 1)

            def from_buf(b):
                return lambda t, m: b[:, t, m * P:(m + 1) * P]

            def scores(g, c):
                n = g * NCHUNK + c
                if c == 0:
                    pe.wait_ge(t_free, g * 2 + (T_STAGE1 + 1))
                if later(n):
                    pe.wait_ge(exp_done, n)
                k0, kn, _ = KEYS[c]
                for pair in range(4):
                    last = nc.tensor.matmul(sps[:, pair, 0:kn], qbd[:, pair, c, :],
                                            kT[:, ds(g, 1), k0:k0 + kn].rearrange("p a n -> p (a n)"),
                                            start=True, stop=True)
                last.then_inc(s_full, 1)

            def prob_transposes(g, c):
                n = g * NCHUNK + c
                pe.wait_ge(p_ready, n + 1)
                if later(n):
                    pe.wait_ge(att_lo, n)
                for pair in range(4):
                    last = nc.tensor.transpose(pps[:, pair, :], prob[:, pair, :], ident)
                last.then_inc(pt_full, 1)

            def attend(g, c):
                if c == 0:
                    pe.wait_ge(vst_ready, g + 1)
                pe.wait_ge(pt_ready, g * NCHUNK + c + 1)
                nc.tensor.matmul(pps[:].rearrange(flat), vst[:, KEYS[c][2], :], probT[:].rearrange(flat),
                                 start=True, stop=True).then_inc(av_full, 1)

            pe.wait_ge(const_full, 16)

            def from_x(g):
                return lambda t, m: xin[:, t, (GCH * g + m) * P:(GCH * g + m + 1) * P]

            pe.wait_ge(x_full[0], 16)
            transposes(T_X, from_x(0))
            for g in range(GROUPS):
                if g + 1 < GROUPS:
                    pe.wait_ge(x_full[g + 1], 16)
                    transposes(T_X + g + 1, from_x(g + 1))
                pe.wait_ge(hT_ready, g + 1)
                gemm(Block(0), ta_hi, ta_lo, 2 * g, 2 * g + 2)

            def tail_a(g, B, hi, lo):
                gemm(B, hi, lo, 0, 1)
                attend(g, 0)
                gemm(B, hi, lo, 1, 4)
                prob_transposes(g, 1)
                scores(g, 2)
                gemm(B, hi, lo, 4, 5)
                attend(g, 1)
                pe.wait_ge(rope_ready, g + 1)
                transposes(g * 2 + T_STAGE1 + 1, from_buf(buf[1]))
                gemm(B, hi, lo, 5, 7)
                prob_transposes(g, 2)
                scores(g, 3)
                gemm(B, hi, lo, 7, 8)
                attend(g, 2)

            def stage1(j, first):
                A, R = Block(B1, 2, j), Block(B1 + 1, 2, j)
                if first:
                    gemm(A, ta_hi, ta_lo, 0, 4)
                    pe.wait_ge(evacuated[0], 1)
                    transposes(T_K, from_buf(buf[1]))
                    gemm(A, ta_hi, ta_lo, 4, 8)
                else:
                    tail_a(j - 1, A, ta_hi, ta_lo)
                gemm(R, ta_hi, ta_lo, 0, 2)
                pe.wait_ge(evacuated[1], A.turn + 1)
                transposes(j * 2 + T_STAGE1, from_buf(buf[0]))
                gemm(R, ta_hi, ta_lo, 2, 3)
                if not first:
                    prob_transposes(j - 1, 3)
                gemm(R, ta_hi, ta_lo, 3, 4)
                if not first:
                    attend(j - 1, 3)
                scores(j, 0)
                gemm(R, ta_hi, ta_lo, 4, 8)
                prob_transposes(j, 0)
                scores(j, 1)

            stage1(0, True)
            with pe.Fori(1, 4) as j:
                stage1(j, False)

            tail_a(3, Block(B2), ta_hi, ta_lo)
            gemm(Block(B2 + 1), tb_hi, tb_lo, 0, 3)
            prob_transposes(3, 3)
            gemm(Block(B2 + 1), tb_hi, tb_lo, 3, 4)
            attend(3, 3)
            gemm(Block(B2 + 1), tb_hi, tb_lo, 4, 6)
            pe.wait_ge(att_lo, 16)
            gemm(Block(B2 + 1), tb_hi, tb_lo, 6, 8)
            with pe.Fori(1, 4) as j:
                gemm(Block(B2, 2, j), ta_hi, ta_lo, 0, 8)
                gemm(Block(B2 + 1, 2, j), tb_hi, tb_lo, 0, 8)

            def stage3(j, first):
                V, G = Block(B3, 2, j), Block(B3 + 1, 2, j)
                gemm(V, ta_hi, ta_lo, 0, 4)
                if not first:
                    pe.wait_ge(gated_ready, j)
                    transposes(j * 2 + T_STAGE3 - 1, from_buf(buf[3]))
                gemm(V, ta_hi, ta_lo, 4, 8)
                gemm(G, ta_hi, ta_lo, 0, 2)
                pe.wait_ge(kst_ready, j + 1)
                if not first:
                    pe.wait_ge(ptr_ready, j * 2)
                for i in range(2):
                    q = qkT[:, ds(j * 2 + i, 1), :].rearrange("p a n -> p (a n)")
                    nc.tensor.matmul(rs_ps[i][:, 0:S], kst[:, i, 0:P], q, start=True, stop=True)
                    nc.tensor.matmul(rs_ps[i][:, S:RET_COLS], kst[:, i, P:S],
                                     qkT[:, ds(j * 2 + i, 1), P:S].rearrange("p a n -> p (a n)"),
                                     start=True, stop=True).then_inc(rs_full, 1)
                gemm(G, ta_hi, ta_lo, 2, 5)
                pe.wait_ge(evacuated[1], V.turn + 1)
                pe.wait_ge(ptr_ready, j * 2 + 2)
                pe.wait_ge(t_free, j * 2 + T_STAGE3)
                for i in range(2):
                    v = [buf[0][:, t, i * RET_V:(i + 1) * RET_V] for t in range(TILES)]
                    nc.tensor.matmul(out_ps[:, i, 0, :], ptr[:, i, 0:P], v[0], start=True, stop=True)
                    nc.tensor.matmul(out_ps[:, i, 1, :], ptr[:, i, P:S], v[0], start=True, stop=False)
                    last = nc.tensor.matmul(out_ps[:, i, 1, :], ptr[:, i, S:RET_COLS], v[1], start=False, stop=True)
                last.then_inc(t_full, 1)
                gemm(G, ta_hi, ta_lo, 5, 8)

            stage3(0, True)
            with pe.Fori(1, 4) as j:
                stage3(j, False)

            def stage4(j, first):
                gemm(Block(B4, 2, j), ta_hi, ta_lo, 0, 3)
                if first:
                    pe.wait_ge(gated_ready, 4)
                    transposes(T_STAGE3 + 7, from_buf(buf[3]))
                else:
                    pe.wait_ge(m_ready, j)
                    transposes(j + (T_STAGE4 - 1), from_buf(buf[3]))
                gemm(Block(B4, 2, j), ta_hi, ta_lo, 3, 8)
                if first:
                    pe.wait_ge(retT_ready, 4)
                gemm(Block(B4 + 1, 2, j), tb_hi, tb_lo, 0, 8)

            stage4(0, True)
            with pe.Fori(1, 4) as j:
                stage4(j, False)

            def from_residual(j):
                return lambda t, m: mix[:, t, (GCH * j + m) * P:(GCH * j + m + 1) * P]

            for j in range(GROUPS):
                if j == 0:
                    pe.wait_ge(t_free, T_STAGE4 + 3)
                gemm(Block(B5 + j), tc_hi, tc_lo, 0, 3)
                if j == 0:
                    pe.wait_ge(m_ready, 4)
                    transposes(T_STAGE4 + 3, from_buf(buf[3]))
                else:
                    prev = Block(B5 + j - 1)
                    pe.wait_ge(evacuated[prev.parity], prev.turn + 1)
                    transposes(T_STAGE5 + j - 1, from_residual(j - 1))
                gemm(Block(B5 + j), tc_hi, tc_lo, 3, 6)
                if j == 0:
                    pe.wait_ge(t_free, T_STAGE4 + 4)
                gemm(Block(B5 + j), tc_hi, tc_lo, 6, 8)

            def stage6(q, first):
                B = [Block(B6 + i, 8, q) for i in range(8)]
                if first:
                    pe.wait_ge(h2T_ready, 3)
                    gemm(B[0], ta_hi, ta_lo, 0, 3)
                    prev = Block(B6 - 1)
                    pe.wait_ge(evacuated[prev.parity], prev.turn + 1)
                    transposes(T_STAGE5 + 3, from_residual(3))
                    gemm(B[0], ta_hi, ta_lo, 3, 6)
                    pe.wait_ge(h2T_ready, 4)
                    gemm(B[0], ta_hi, ta_lo, 6, 8)
                else:
                    gemm(B[0], ta_hi, ta_lo, 0, 8)
                for i in range(1, 5):
                    hi, lo = (ta_hi, ta_lo) if i < 4 else (tb_hi, tb_lo)
                    if i == 4:
                        pe.wait_ge(t_free, q * 4 + (T_STAGE6 + 3))
                    gemm(B[i], hi, lo, 0, 3)
                    pe.wait_ge(u_ready, q * 4 + i)
                    transposes(q * 4 + (T_STAGE6 + i - 1), from_buf(buf[0]))
                    gemm(B[i], hi, lo, 3, 6)
                    if i == 4:
                        pe.wait_ge(t_free, q * 4 + (T_STAGE6 + 4))
                    gemm(B[i], hi, lo, 6, 8)
                for i in range(5, 8):
                    gemm(B[i], tb_hi, tb_lo, 0, 8)

            stage6(0, True)
            with pe.Fori(1, 4) as q:
                stage6(q, False)

        @block.scalar
        def _(act):
            def split(B, u0, u1):
                for u in range(u0, u1):
                    if u % 2 == 0:
                        act.wait_ge(raw_full[u // 2], B.number * 16 + 16)
                    if not B.very_first or u >= 4:
                        act.wait_ge(unit_done, B.unit(u - 4))
                    s = u * UCH % (KCH // 2)
                    nc.scalar.activation(whi[:, s:s + UCH, :], raw[:, u * UCH:(u + 1) * UCH, :],
                                         ACT.Copy).then_inc(hi_ready, 1)

            def scaled(B, dst, func, scale):
                act.wait_ge(unit_done, B.unit(UNITS - 1))
                for t in range(TILES):
                    last = nc.scalar.activation(dst[:, t, :], acc[B.parity][:, t, :], func, scale=scale[:, t:t + 1])
                return last

            def hi_from_psum(turn, dst, g):
                act.wait_ge(t_full, turn + 1)
                nc.scalar.activation(dst[:, ds(g * GCH, GCH), :], tps[:], ACT.Copy).then_inc(t_hi, 1)

            def hi_from_gained(turn, src, dst, g):
                act.wait_ge(t_free, turn + 1)
                nc.scalar.activation(dst[:, ds(g * GCH, GCH), :], src[:].rearrange("p t (k n) -> p (t k) n", n=S),
                                     ACT.Copy).then_inc(t_hi, 1)

            def exps(g, c):
                n = g * NCHUNK + c
                kn = KEYS[c][1]
                act.wait_ge(negm_ready, n + 1)
                if later(n):
                    act.wait_ge(pt_full, n)
                for pair in range(4):
                    nc.scalar.activation(prob[:, pair, 0:kn], sps[:, pair, 0:kn], ACT.Exp, scale=ATT_SCALE,
                                         bias=negm[:, pair:pair + 1], accum_out=sums[:, pair:pair + 1])
                nc.scalar.activation(es[:], esd[:], ACT.Exp).then_inc(exp_done, 1)

            def probs_out(g, c):
                n = g * NCHUNK + c
                act.wait_ge(pt_full, n + 1)
                if later(n):
                    act.wait_ge(av_full, n)
                nc.scalar.activation(probT[:], pps[:], ACT.Copy).then_inc(pt_ready, 1)

            def attended_hi(g, c):
                act.wait_ge(av_full, g * NCHUNK + c + 1)
                v = pps[:].rearrange("p a (h q) -> p a h q", h=2)
                for h in range(2):
                    part = slice(h * 64, h * 64 + 64)
                    last = nc.scalar.activation(tb_hi[part, ds(g * GCH, GCH), c * CHUNK:(c + 1) * CHUNK],
                                                v[part, :, h, :], ACT.Copy)
                last.then_inc(att_hi, 1)

            act.dma_start(small[:], small_c).then_inc(const_full, 16)

            B = Block(0)
            for g in range(GROUPS):
                split(B, 2 * g, 2 * g + 1)
                hi_from_gained(T_X + g, buf[2 + g % 2], ta_hi, g)
                split(B, 2 * g + 1, 2 * g + 2)
                if g >= 2:
                    if g == 2:
                        for ready in x_full:
                            act.wait_ge(ready, 16)
                    else:
                        act.wait_ge(ssq_ready, 1)
                    g -= 2
                    nc.scalar.activation(junk[:], xin[:, g, :], ACT.Square, accum_out=ssq[:, g:g + 1]).then_inc(ssq_ready, 1)

            def tail_a(g, B):
                split(B, 0, 1)
                exps(g, 0)
                split(B, 1, 4)
                probs_out(g, 0)
                split(B, 4, 5)
                exps(g, 1)
                attended_hi(g, 0)
                split(B, 5, 8)
                probs_out(g, 1)

            def tail_r(g, B):
                split(B, 0, 1)
                exps(g, 2)
                attended_hi(g, 1)
                split(B, 1, 3)
                probs_out(g, 2)
                split(B, 3, 4)
                exps(g, 3)
                attended_hi(g, 2)

            def stage1(j, first):
                A, R = Block(B1, 2, j), Block(B1 + 1, 2, j)
                if first:
                    split(A, 0, 4)
                    act.wait_ge(rstd_ready, 1)
                    act.wait_ge(unit_done, Block(0).unit(UNITS - 1))
                    kd = buf[1][:].rearrange("p t (g e d) -> p t g e d", e=2, d=ATT_D)
                    vd = vwin[:].rearrange("p w g (e d) -> p w g e d", e=2)
                    for t in range(TILES):
                        kv = acc[0][:, t, :].rearrange("p (s g d) -> p s g d", s=2, d=ATT_D)
                        for e in range(2):
                            nc.scalar.activation(kd[:, t, :, e, :], kv[:, 0], ACT.Copy, scale=rstd[:, t:t + 1])
                            last = nc.scalar.activation(vd[:, 2 * t, :, e, :], kv[:, 1], ACT.Copy, scale=rstd[:, t:t + 1])
                    last.then_inc(evacuated[0], 1)
                    split(A, 4, 8)
                    act.wait_ge(t_full, T_K + 1)
                    nc.scalar.activation(kT[:], tps[:], ACT.Copy).then_inc(t_free, 1)
                    split(R, 0, 4)
                else:
                    tail_a(j - 1, A)
                    tail_r(j - 1, R)
                    act.wait_ge(t_full, j * 2 + (T_STAGE1 - 1))
                scaled(A, buf[0], ACT.Copy, rstd).then_inc(evacuated[1], 1)
                split(R, 4, 6)
                act.wait_ge(t_full, j * 2 + (T_STAGE1 + 1))
                act.wait_ge(consts_ready, 1)
                for h in range(2):
                    part = slice(h * 64, h * 64 + 64)
                    last = nc.scalar.activation(qbd[part, :, :, part], tps[part, :, :].rearrange("p a (c q) -> p a c q", q=CHUNK),
                                                ACT.Copy)
                last.then_inc(t_free, 1)
                split(R, 6, 7)
                if not first:
                    probs_out(j - 1, 3)
                split(R, 7, 8)
                if not first:
                    attended_hi(j - 1, 3)

            stage1(0, True)
            with act.Fori(1, 4) as j:
                stage1(j, False)

            tail_a(3, Block(B2))
            tail_r(3, Block(B2 + 1))
            act.wait_ge(rope_ready, 4)
            scaled(Block(B2), buf[2], ACT.Tanh, rstd_half).then_inc(evacuated[1], 1)
            split(Block(B2 + 1), 4, 7)
            probs_out(3, 3)
            split(Block(B2 + 1), 7, 8)
            attended_hi(3, 3)
            with act.Fori(1, 4) as j:
                G, A = Block(B2, 2, j), Block(B2 + 1, 2, j)
                split(G, 0, 8)
                split(A, 0, 4)
                act.wait_ge(evacuated[0], A.turn)
                scaled(G, buf[2], ACT.Tanh, rstd_half).then_inc(evacuated[1], 1)
                split(A, 4, 8)

            def retention_squares(j, B):
                act.wait_ge(t_full, j * 2 + (T_STAGE3 + 1))
                if later(j):
                    act.wait_ge(rms_ready, j)
                for i in range(2):
                    for t in range(TILES):
                        last = nc.scalar.activation(junk3[:, i, t, :], out_ps[:, i, t, :], ACT.Square,
                                                    accum_out=ssqr[:, i, t:t + 1])
                last.then_inc(rssq_ready, 1)

            junk3 = buf[3][:].rearrange("p t (i e) -> p i t e", i=2)

            def tail3(j, B):
                split(B, 0, 1)
                if later(j):
                    act.wait_ge(t_full, j * 2 + T_STAGE3)
                retention_squares(j, B)
                split(B, 1, 4)
                if later(j):
                    act.wait_ge(retT_ready, j)
                else:
                    act.wait_ge(evacuated[0], Block(B3 - 1).turn + 1)
                scaled(Block(B3 + 1, 2, j), buf[2], ACT.Tanh, rstd_half).then_inc(rgate_ready, 1)
                split(B, 4, 8)
                hi_from_gained(j * 2 + (T_STAGE3 + 1), buf[2], tb_hi, j)

            def stage3(j, first):
                V, G = Block(B3, 2, j), Block(B3 + 1, 2, j)
                if first:
                    split(V, 0, 8)
                    act.wait_ge(t_free, T_STAGE1 + 8)
                else:
                    tail3(j - 1, V)
                    act.wait_ge(rs_full, j * 2)
                nc.scalar.activation(kst[:], qkT[:, ds(j * 2 + RET_HEADS, 2), :], ACT.Copy).then_inc(kst_ready, 1)
                split(G, 0, 4)
                if not first:
                    act.wait_ge(t_full, j * 2 + (T_STAGE3 - 1))
                scaled(V, buf[0], ACT.Copy, rstd).then_inc(evacuated[1], 1)
                split(G, 4, 8)

            stage3(0, True)
            with act.Fori(1, 4) as j:
                stage3(j, False)

            def stage4(j, first):
                G, R = Block(B4, 2, j), Block(B4 + 1, 2, j)
                if first:
                    tail3(3, G)
                else:
                    split(G, 0, 7)
                    hi_from_psum(j + (T_STAGE4 - 1), tc_hi, j - 1)
                    split(G, 7, 8)
                split(R, 0, 4)
                if first:
                    act.wait_ge(retT_ready, 4)
                else:
                    act.wait_ge(evacuated[0], R.turn)
                scaled(G, buf[2], ACT.Tanh, rstd_half).then_inc(evacuated[1], 1)
                split(R, 4, 8)

            stage4(0, True)
            with act.Fori(1, 4) as j:
                stage4(j, False)

            def residual_squares(B, j, done):
                act.wait_ge(evacuated[B.parity], B.turn + 1)
                for t in range(TILES):
                    last = nc.scalar.activation(buf[3][:, t, :], mix[:, t, j * COLS:(j + 1) * COLS], ACT.Square,
                                                accum_out=ssq2[:, t, j:j + 1])
                last.then_inc(done, 1)

            for j in range(GROUPS + 1):
                B = Block(B5 + j)
                split(B, 0, 5)
                if j:
                    if j == 1:
                        act.wait_ge(t_full, T_STAGE4 + 4)
                    residual_squares(Block(B5 + j - 1), j - 1, x1_sq)
                split(B, 5, 7)
                if j == 0:
                    hi_from_psum(T_STAGE4 + 3, tc_hi, 3)
                else:
                    hi_from_gained(T_STAGE5 + j - 1, buf[2], ta_hi, j - 1)
                split(B, 7, 8)

            def stage6(q, first):
                B = [Block(B6 + i, 8, q) for i in range(8)]
                if not first:
                    split(B[0], 0, 5)
                    residual_squares(Block(B6 - 1, 8, q), 3, down_sq)
                    split(B[0], 5, 8)
                for i in range(1, 5):
                    split(B[i], 0, 4)
                    if first and i == 1:
                        act.wait_ge(rstd2_ready, 1)
                    else:
                        act.wait_ge(t_full, q * 4 + (T_STAGE6 + i - 1))
                    scaled_relu(B[i - 1])
                    split(B[i], 4, 7)
                    hi_from_psum(q * 4 + (T_STAGE6 + i - 1), tb_hi, i - 1)
                    split(B[i], 7, 8)
                for i in range(5, 8):
                    split(B[i], 0, 5)
                    residual_squares(B[i - 1], i - 5, down_sq)
                    split(B[i], 5, 8)

            def scaled_relu(B):
                scaled(B, buf[0], ACT.Relu, rstd2).then_inc(evacuated[B.parity], 1)

            stage6(0, True)
            with act.Fori(1, 4) as q:
                stage6(q, False)
            residual_squares(Block(68), 3, down_sq)
            act.wait_ge(rstd3_ready, 1)
            act.wait_ge(final_g, 2)
            for h in range(2):
                cols = slice(h * 1024, (h + 1) * 1024)
                nc.scalar.activation(final[:, 0, cols], final[:, 0, cols], ACT.Copy, scale=rstd3[:, 0:1]).then_inc(final_act, 1)

        @block.vector
        def _(dve):
            V_ = nc.vector
            mine = Steps(own)

            def split(B, u0, u1):
                for u in range(u0, u1):
                    dve.wait_ge(hi_ready, B.unit(u))
                    s = u * UCH % (KCH // 2)
                    V_.tensor_tensor(wlo[:, s:s + UCH, :], raw[:, u * UCH:(u + 1) * UCH, :],
                                     whi[:, s:s + UCH, :].bitcast(f32), ALU.subtract).then_inc(lo_ready, 1)

            def gain(turn, dst, gains, g):
                dve.wait_ge(t_full, turn + 1)
                gsl = gains[:, ds(g * GCH, GCH)].unsqueeze(2).to_broadcast([P, GCH, S])
                V_.tensor_tensor(dst[:].rearrange("p t (k n) -> p (t k) n", n=S), tps[:], gsl, ALU.mult).then_inc(t_free, 1)

            def lo_from_gained(n, src, hi, lo, g, done):
                dve.wait_ge(t_hi, n)
                V_.tensor_tensor(lo[:, ds(g * GCH, GCH), :], src[:].rearrange("p t (k n) -> p (t k) n", n=S),
                                 hi[:, ds(g * GCH, GCH), :].bitcast(f32), ALU.subtract).then_inc(done, 1)

            def lo_from_psum(n, hi, lo, g):
                dve.wait_ge(t_hi, n)
                V_.tensor_tensor(lo[:, ds(g * GCH, GCH), :], tps[:], hi[:, ds(g * GCH, GCH), :].bitcast(f32),
                                 ALU.subtract).then_inc(t_free, 1)

            V_.memset(qbd[:], 0.0).then_inc(consts_ready, 1)
            dve.wait_ge(const_full, 16)
            mine.step(V_.tensor_scalar(nsink[:], sink, -1.0, None, ALU.mult))
            B = Block(0)
            gain(T_X, buf[2], gmix, 0)
            for g in range(GROUPS):
                split(B, 2 * g, 2 * g + 1)
                lo_from_gained(g + 1, buf[2 + g % 2], ta_hi, ta_lo, g, hT_ready)
                if g + 1 < GROUPS:
                    if g >= 1:
                        dve.wait_ge(hT_ready, g)
                    gain(T_X + g + 1, buf[2 + (g + 1) % 2], gmix, g + 1)
                split(B, 2 * g + 1, 2 * g + 2)
            dve.wait_ge(ssq_ready, 2)
            V_.tensor_scalar(msq[:, 0:2], ssq[:], 1.0 / D, EPS, ALU.mult, ALU.add).then_inc(ms_ready, 1)
            dve.wait_ge(pow_ready, 1)
            V_.tensor_scalar(rstd_half[:], rstd[:], 0.5, None, ALU.mult).then_inc(rstd_ready, 1)
            mine.step(V_.tensor_tensor(roper[:], rope,
                                       rstd[:].unsqueeze(1).unsqueeze(3).to_broadcast([P, 2, TILES, RET_QK // 2]), ALU.mult))

            def maxima(g, c):
                n = g * NCHUNK + c
                dve.wait_ge(s_full, n + 1)
                if later(n):
                    dve.wait_ge(exp_done, n)
                mine.step(V_.tensor_reduce(mx[:], sps[:, :, 0:KEYS[c][1]], AX.X, ALU.max))
                mine.wait(dve)
                mine.step(V_.scalar_tensor_tensor(negm[:], mx[:], -ATT_SCALE, nsink[:, ds(g * 4, 4)], ALU.mult, ALU.min))
                mine.wait(dve)
                V_.tensor_tensor(esd[:], negm[:], nsink[:, ds(g * 4, 4)], ALU.subtract).then_inc(negm_ready, 1)

            def normalise(g, c):
                n = g * NCHUNK + c
                kn = KEYS[c][1]
                dve.wait_ge(exp_done, n + 1)
                mine.step(V_.tensor_tensor(den[:], sums[:], es[:], ALU.add))
                mine.wait(dve)
                mine.step(V_.reciprocal(rden[:], den[:]))
                if c == 0:
                    mine.step(V_.memset(prob[:, :, kn:P], 0.0))
                mine.wait(dve)
                V_.tensor_tensor(prob[:, :, 0:kn], prob[:, :, 0:kn], rden[:].unsqueeze(2).to_broadcast([P, 4, kn]),
                                 ALU.mult).then_inc(p_ready, 1)

            def attended_lo(g, c):
                dve.wait_ge(att_hi, g * NCHUNK + c + 1)
                v = pps[:].rearrange("p a (h q) -> p a h q", h=2)
                for h in range(2):
                    part = slice(h * 64, h * 64 + 64)
                    at = (part, ds(g * GCH, GCH), slice(c * CHUNK, (c + 1) * CHUNK))
                    last = V_.tensor_tensor(tb_lo[at], v[part, :, h, :], tb_hi[at].bitcast(f32), ALU.subtract)
                last.then_inc(att_lo, 1)

            def rotate(g, B):
                dve.wait_ge(unit_done, B.unit(UNITS - 1))
                half = RET_QK // 2
                v = acc[B.parity][:].rearrange("p t (h x d) -> p t h x d", x=2, d=half)
                cos = roper[:, 0].unsqueeze(2).to_broadcast([P, TILES, 4, half])
                sin = roper[:, 1].unsqueeze(2).to_broadcast([P, TILES, 4, half])
                o = buf[1][:].rearrange("p t (h x d) -> p t h x d", x=2, d=half)
                tmp = [b[:].rearrange("p t (h d) -> p t h d", d=half)[:, :, 4 * i:4 * i + 4, :]
                       for b in (buf[2], buf[3]) for i in range(2)]
                V_.tensor_tensor(tmp[0], v[:, :, :, 0, :], cos, ALU.mult)
                V_.tensor_tensor(tmp[1], v[:, :, :, 1, :], sin, ALU.mult)
                mine.step(V_.tensor_tensor(tmp[2], v[:, :, :, 1, :], cos, ALU.mult))
                V_.tensor_tensor(tmp[3], v[:, :, :, 0, :], sin, ALU.mult).then_inc(evacuated[B.parity], 1)
                dve.wait_ge(t_full, g * 2 + T_STAGE1)
                dve.wait_ge(evacuated[B.parity], B.turn + 1)
                V_.tensor_tensor(o[:, :, :, 0, :], tmp[0], tmp[1], ALU.subtract)
                V_.tensor_tensor(o[:, :, :, 1, :], tmp[2], tmp[3], ALU.add).then_inc(rope_ready, 1)

            def tail_a(g, B, R):
                split(B, 0, 2)
                normalise(g, 0)
                split(B, 2, 4)
                maxima(g, 1)
                rotate(g, R)
                split(B, 4, 6)
                normalise(g, 1)
                attended_lo(g, 0)
                split(B, 6, 8)
                maxima(g, 2)

            def tail_r(g, B):
                split(B, 0, 1)
                dve.wait_ge(t_full, g * 2 + (T_STAGE1 + 2))
                V_.tensor_copy(qkT[:, ds(g * 4, 4), :], tps[:]).then_inc(t_free, 1)
                split(B, 1, 2)
                normalise(g, 2)
                attended_lo(g, 1)
                split(B, 2, 3)
                maxima(g, 3)
                split(B, 3, 5)
                normalise(g, 3)
                attended_lo(g, 2)

            def stage1(j, first):
                A, R = Block(B1, 2, j), Block(B1 + 1, 2, j)
                if first:
                    split(A, 0, 4)
                    dve.wait_ge(evacuated[0], 1)
                    V_.tensor_copy(vwin[0:64, 1], vwin[64:128, 0])
                    V_.tensor_copy(vwin[64:128, 1], vwin[0:64, 2]).then_inc(vshift, 1)
                    split(A, 4, 8)
                    split(R, 0, 5)
                else:
                    tail_a(j - 1, A, Block(B1 + 1, 2, j - 1))
                    tail_r(j - 1, R)
                split(R, 5, 8)
                if not first:
                    attended_lo(j - 1, 3)
                maxima(j, 0)

            stage1(0, True)
            mine_at = OWN_STAGE1
            with dve.Fori(1, 4) as j:
                mine.enter_loop(j, 1, mine_at)
                stage1(j, False)
            mine.leave_loop(3, mine_at)

            def gate(B):
                dve.wait_ge(evacuated[1], B.turn + 1)
                mine.step(V_.tensor_scalar(buf[2][:], buf[2][:], 0.5, 0.5, ALU.mult, ALU.add))

            def gated_attention(j):
                B = Block(B2 + 1, 2, j)
                dve.wait_ge(unit_done, B.unit(UNITS - 1))
                mine.wait(dve)
                V_.tensor_tensor(mix[:, :, ds(j * COLS, COLS)], buf[2][:], acc[0][:], ALU.mult).then_inc(evacuated[0], 1)

            tail_a(3, Block(B2), Block(B2 - 1))
            tail_r(3, Block(B2 + 1))
            gate(Block(B2))
            split(Block(B2 + 1), 5, 8)
            attended_lo(3, 3)
            with dve.Fori(1, 4) as j:
                mine.enter_loop(j, 1, OWN_STAGE2)
                split(Block(B2, 2, j), 0, 4)
                gated_attention(j - 1)
                split(Block(B2, 2, j), 4, 8)
                split(Block(B2 + 1, 2, j), 0, 5)
                gate(Block(B2, 2, j))
                split(Block(B2 + 1, 2, j), 5, 8)
            mine.leave_loop(3, OWN_STAGE2)

            def tail3(j, B):
                split(B, 0, 2)
                dve.wait_ge(rssq_ready, j + 1)
                V_.tensor_scalar(msq[:], ssqr[:].rearrange("p i t -> p (i t)"), 1.0 / RET_V, EPS, ALU.mult, ALU.add).then_inc(rms_ready, 1)
                split(B, 2, 3)
                dve.wait_ge(rpow_ready, j + 1)
                mine.step(V_.tensor_tensor(retsc[:], powr[:], rstd_half[:].unsqueeze(1).to_broadcast([P, 2, TILES]), ALU.mult))
                mine.wait(dve)
                V_.tensor_tensor(buf[1][:].rearrange("p t (i e) -> p i t e", i=2), out_ps,
                                 retsc[:].unsqueeze(3).to_broadcast([P, 2, TILES, RET_V]), ALU.mult).then_inc(t_free, 1)
                split(B, 3, 4)
                dve.wait_ge(rgate_ready, j + 1)
                dve.wait_ge(t_free, j * 2 + (T_STAGE3 + 1))
                V_.tensor_tensor(buf[3][:], buf[1][:], acc[0][:], ALU.mult).then_inc(evacuated[0], 1)
                dve.wait_ge(evacuated[0], Block(B3 + 1, 2, j).turn + 1)
                V_.scalar_tensor_tensor(buf[3][:].rearrange(flat), buf[2][:].rearrange(flat), 1.0,
                                        buf[3][:].rearrange(flat), ALU.add, ALU.mult).then_inc(gated_ready, 1)
                split(B, 4, 8)
                dve.wait_ge(gated_ready, j + 1)
                gain3(j)

            def gain3(j):
                dve.wait_ge(t_full, j * 2 + (T_STAGE3 + 2))
                gsl = gret[:, ds(j * GCH, GCH)].unsqueeze(2).to_broadcast([P, GCH, S])
                V_.tensor_tensor(buf[2][:].rearrange("p t (k n) -> p (t k) n", n=S), tps[:], gsl, ALU.mult).then_inc(t_free, 1)

            def decayed(j):
                for i in range(2):
                    dve.wait_ge(rs_full, j * 2 + (i + 1))
                    V_.tensor_tensor(ptr[:, i, :], rs_ps[i][:, 0:RET_COLS], decay[:, ds(j * 2 + i, 1), :].rearrange("p a n -> p (a n)"),
                                     ALU.mult).then_inc(ptr_ready, 1)

            def stage3(j, first):
                V, G = Block(B3, 2, j), Block(B3 + 1, 2, j)
                if first:
                    split(V, 0, 4)
                    gated_attention(3)
                    split(V, 4, 8)
                    dve.wait_ge(decay_full, 16)
                    split(G, 0, 1)
                else:
                    tail3(j - 1, V)
                    split(G, 0, 1)
                    lo_from_gained(j + 4, buf[2], tb_hi, tb_lo, j - 1, retT_ready)
                split(G, 1, 6)
                decayed(j)
                split(G, 6, 8)

            stage3(0, True)
            with dve.Fori(1, 4) as j:
                mine.enter_loop(j, 1, OWN_STAGE3)
                stage3(j, False)
            mine.leave_loop(3, OWN_STAGE3)

            def merge(j):
                B = Block(B4 + 1, 2, j)
                dve.wait_ge(unit_done, B.unit(UNITS - 1))
                mine.wait(dve)
                dve.wait_ge(t_full, j + T_STAGE4)
                V_.tensor_tensor(buf[3][:], buf[2][:], acc[0][:], ALU.mult).then_inc(evacuated[0], 1)
                dve.wait_ge(evacuated[0], B.turn + 1)
                V_.tensor_tensor(buf[3][:], buf[3][:], mix[:, :, ds(j * COLS, COLS)], ALU.add).then_inc(m_ready, 1)

            def stage4(j, first):
                G, R = Block(B4, 2, j), Block(B4 + 1, 2, j)
                if first:
                    tail3(3, G)
                    split(R, 0, 1)
                    lo_from_gained(8, buf[2], tb_hi, tb_lo, 3, retT_ready)
                else:
                    split(G, 0, 4)
                    merge(j - 1)
                    split(G, 4, 8)
                    lo_from_psum(j + 8, tc_hi, tc_lo, j - 1)
                    split(R, 0, 1)
                split(R, 1, 5)
                gate(G)
                split(R, 5, 8)

            stage4(0, True)
            with dve.Fori(1, 4) as j:
                mine.enter_loop(j, 1, OWN_STAGE4)
                stage4(j, False)
            mine.leave_loop(3, OWN_STAGE4)

            def add_residual(B, j):
                dve.wait_ge(unit_done, B.unit(UNITS - 1))
                sl = mix[:, :, j * COLS:(j + 1) * COLS]
                V_.tensor_tensor(sl, sl, acc[B.parity][:], ALU.add).then_inc(evacuated[B.parity], 1)

            def inverse_rms(done):
                mine.step(V_.tensor_reduce(sum2[:], ssq2[:], AX.X, ALU.add))
                mine.wait(dve)
                V_.tensor_scalar(msq[:, 0:2], sum2[:], 1.0 / D, EPS, ALU.mult, ALU.add).then_inc(done, 1)

            for j in range(GROUPS + 1):
                B = Block(B5 + j)
                split(B, 0, 4)
                if j == 0:
                    merge(3)
                else:
                    dve.wait_ge(xres_full[j - 1], 16)
                    add_residual(Block(B5 + j - 1), j - 1)
                split(B, 4, 7)
                if j:
                    gain(T_STAGE5 + j - 1, buf[2], gffn, j - 1)
                split(B, 7, 8)
                if j:
                    lo_from_gained(12 + j, buf[2], ta_hi, ta_lo, j - 1, h2T_ready)
                else:
                    lo_from_psum(12, tc_hi, tc_lo, 3)
                if j == GROUPS:
                    dve.wait_ge(x1_sq, 4)
                    inverse_rms(ms2_ready)

            def square(n, B):
                dve.wait_ge(evacuated[B.parity], B.turn + 1)
                V_.tensor_tensor(buf[0][:], buf[0][:], buf[0][:], ALU.mult).then_inc(u_ready, 1)

            def add_down(q, i, B):
                if later(q):
                    dve.wait_ge(down_sq, q * 4 + (i - 3))
                add_residual(B, i)

            def stage6(q, first):
                B = [Block(B6 + i, 8, q) for i in range(8)]
                if not first:
                    split(B[0], 0, 4)
                    add_residual(Block(B6 - 1, 8, q), 3)
                    split(B[0], 4, 8)
                for i in range(1, 5):
                    split(B[i], 0, 5)
                    square(q * 4 + i, B[i - 1])
                    split(B[i], 5, 8)
                    lo_from_psum(q * 4 + (16 + i), tb_hi, tb_lo, i - 1)
                for i in range(5, 8):
                    split(B[i], 0, 4)
                    if not first:
                        dve.wait_ge(down_sq, q * 4 + (i - 8))
                    add_residual(B[i - 1], i - 5)
                    split(B[i], 4, 8)

            stage6(0, True)
            with dve.Fori(1, 4) as q:
                stage6(q, False)
            dve.wait_ge(fin_full, 16)

            def final_gain(j0, j1):
                cols = slice(j0 * COLS, j1 * COLS)
                V_.tensor_tensor(final[:, :, cols], mix[:, :, cols],
                                 gfin[:, cols].unsqueeze(1).to_broadcast([P, TILES, (j1 - j0) * COLS]),
                                 ALU.mult).then_inc(final_g, 1)

            for j in range(3):
                B = Block(B6 + 28 + j)
                dve.wait_ge(evacuated[B.parity], B.turn + 1)
            final_gain(0, 3)
            dve.wait_ge(down_sq, 12)
            add_residual(Block(68), 3)
            dve.wait_ge(evacuated[0], Block(68).turn + 1)
            final_gain(3, 4)
            dve.wait_ge(down_sq, 16)
            inverse_rms(ms3_ready)
            dve.wait_ge(rstd3_ready, 1)
            dve.wait_ge(final_g, 2)
            for h in range(2):
                cols = slice(h * 1024, (h + 1) * 1024)
                V_.tensor_scalar(final[:, 1, cols], final[:, 1, cols], rstd3[:, 1:2], None, ALU.mult).then_inc(final_dve, 1)

        @block.gpsimd
        def _(pool):
            nc.gpsimd.memset(mhalf[:], -0.5).then_inc(mhalf_set, 1)
            pool.wait_ge(mhalf_set, 1)
            pool.wait_ge(ms_ready, 1)
            nc.gpsimd.tensor_tensor(rstd[:], msq[:, 0:2], mhalf[:, 0:2], ALU.pow).then_inc(pow_ready, 1)
            pool.wait_ge(vshift, 1)
            for g in range(KV_HEADS):
                if g:
                    pool.wait_ge(av_full, g * NCHUNK)
                nc.gpsimd.tensor_copy(vst[:], vwin[:, :, g, :]).then_inc(vst_ready, 1)
            for j in range(4):
                pool.wait_ge(rms_ready, j + 1)
                nc.gpsimd.tensor_tensor(powr[:].rearrange("p i t -> p (i t)"), msq[:], mhalf[:], ALU.pow).then_inc(rpow_ready, 1)
            pool.wait_ge(ms2_ready, 1)
            nc.gpsimd.tensor_tensor(rstd2[:], msq[:, 0:2], mhalf[:, 0:2], ALU.pow).then_inc(rstd2_ready, 1)
            pool.wait_ge(ms3_ready, 1)
            nc.gpsimd.tensor_tensor(rstd3[:], msq[:, 0:2], mhalf[:, 0:2], ALU.pow).then_inc(rstd3_ready, 1)


def constants():
    half = RET_QK // 2
    inv = (np.float32(10000.0) ** (-np.arange(half, dtype=np.float32) / np.float32(half))).astype(np.float32)
    ang = np.arange(S, dtype=np.float32)[:, None] * inv[None, :]
    cs = np.stack([np.cos(ang), np.sin(ang)]).astype(np.float32)
    rope = np.ascontiguousarray(cs.reshape(2, TILES, P, half).transpose(2, 0, 1, 3))
    n = np.arange(S)
    lg = np.log1p(-np.exp2(-5.0 - np.arange(RET_HEADS)))
    full = np.exp(lg[:, None, None] * np.abs(n[:, None] - n[None, :])) * RET_QK ** -0.5
    full = full * (n[:, None] // CHUNK <= n[None, :] // CHUNK)
    decay = np.concatenate([full[:, :P, :], full[:, P:, P:]], axis=2).transpose(1, 0, 2)
    return np.eye(P, dtype=np.float32), rope, np.ascontiguousarray(decay.astype(np.float32))


def kernel(x, norm_mix_g, w_in, ret_norm_g, attn_sinks, w_ret_branch, w_attn_branch, w_gate, w_out,
           norm_ffn_g, w_up, w_down, norm_final_g):
    import concourse.bacc as _bacc
    from concourse.bass_utils import run_bass_kernel_spmd as _run

    nc = _bacc.Bacc("TRN2", target_bir_lowering=False, num_devices=1)
    ident, rope, decay = constants()

    def columns(g):
        return np.asarray(g).reshape(KCH, P).T

    sinks = np.repeat(np.asarray(attn_sinks).reshape(16, 2).T, P // 2, axis=0)
    small = np.concatenate([ident, rope.reshape(P, -1), columns(norm_mix_g), columns(ret_norm_g),
                            columns(norm_ffn_g), sinks], axis=1)
    given = {
        "x": np.asarray(x)[0], "w_in": np.asarray(w_in)[0],
        "w_ret": np.asarray(w_ret_branch)[0], "w_att": np.asarray(w_attn_branch)[0],
        "w_gate": np.asarray(w_gate)[0], "w_out": np.asarray(w_out)[0],
        "w_up": np.asarray(w_up)[0], "w_down": np.asarray(w_down)[0],
        "g_fin": np.asarray(norm_final_g), "small_c": small, "decay_c": decay,
    }
    arrays, args = {}, {}
    for name, a in given.items():
        arrays["in_" + name] = np.ascontiguousarray(a)
        args[name] = nc.dram_tensor("in_" + name, a.shape, mybir.dt.float32, kind="ExternalInput").ap()
    out = nc.dram_tensor("out_0", (S, D), mybir.dt.float32, kind="ExternalOutput").ap()
    build(nc, out=out, **args)
    r = _run(nc, [arrays], core_ids=[0])
    return r.results[0]["out_0"].reshape(1, S, D)
```

```python
import concourse.bass as bass
from concourse import mybir
from contextlib import ExitStack
import numpy as np

P = 128
D = 2048
S = 256
TILES = S // P
COLS = 512
KCH = D // P
UNITS = 8
UCH = KCH // UNITS
SQ = 32
LOADS = 4
GROUPS = D // COLS
GCH = COLS // P
EPS = 1e-6
CHUNK = 64
NCHUNK = S // CHUNK
RET_HEADS = 8
RET_QK = D // 16
RET_V = D // 8
ATT_D = 64
KV_HEADS = 4
RET_COLS = S + (S - P)
ATT_SCALE = ATT_D ** -0.5
OFF_RQK = 0
OFF_RV = 2 * RET_HEADS * RET_QK
OFF_RG = OFF_RV + D
OFF_AQ = OFF_RG + D
OFF_AKV = OFF_AQ + D
SMALL = P + 2 * TILES * (RET_QK // 2) + 4 * KCH
KEYS = [(0, CHUNK, 0), (0, 2 * CHUNK, 0), (CHUNK, 2 * CHUNK, 1), (2 * CHUNK, 2 * CHUNK, 2)]


class Block:

    def __init__(self, first, step=0, j=0):
        self.number = j * step + first
        self.parity = first % 2
        self.turn = j * (step // 2) + first // 2
        self.reused = first >= 2
        self.very_first = first == 0

    def unit(self, u):
        return self.number * UNITS + (u + 1)


def later(n):
    return not (type(n) is int and n == 0)


class Steps:

    def __init__(self, sem):
        self.sem, self.base, self.here, self.total = sem, 0, 0, 0

    def step(self, instruction):
        instruction.then_inc(self.sem, 1)
        self.here += 1
        self.total += 1

    def wait(self, engine):
        engine.wait_ge(self.sem, self.base + self.here)

    def enter_loop(self, j, first, per):
        self.before, self.base, self.here = self.total, j * per + (self.total - first * per), 0

    def leave_loop(self, turns, per):
        assert self.here == per, (self.here, per)
        self.total = self.before + turns * per
        self.base, self.here = self.total, 0


WARM_UP = 16
OWN_STAGE1, OWN_STAGE2, OWN_STAGE3, OWN_STAGE4 = 18, 1, 1, 1


def build(nc, x, x_t, w_in, w_ret, w_att, w_gate, w_out, w_up, w_down, g_fin,
          small_c, decay_c, out):
    f32, f32r = mybir.dt.float32, mybir.dt.float32r
    ALU, ACT, AX = mybir.AluOpType, mybir.ActivationFunctionType, mybir.AxisListType
    ds = bass.ds

    ctx = ExitStack()
    with ctx:
        here = [(nc.sbuf_base + 63) // 64 * 64]

        def place(name, shape, dt, at=None):
            size = int(np.prod(shape[1:])) * 4
            if at is None:
                at = here[0]
                here[0] += (size + 31) // 32 * 32
            return nc.alloc_sbuf_tensor_at(name, shape, dt, offset=at)

        def sem(name):
            return ctx.enter_context(nc.semaphore(name))

        K = 1024
        at_a = here[0]
        ta_hi = place("ta_hi", [P, KCH, S], f32r)
        ta_lo = place("ta_lo", [P, KCH, S], f32r)
        at_b = here[0]
        tb_hi = place("tb_hi", [P, KCH, S], f32r)
        tb_lo = place("tb_lo", [P, KCH, S], f32r)
        at_c = here[0]
        tc_hi = place("tc_hi", [P, KCH, S], f32r)
        tc_lo = place("tc_lo", [P, KCH, S], f32r)
        at_m = here[0]
        mix = place("mix", [P, TILES, D], f32)
        raw = place("raw", [P, KCH, COLS], f32)
        whi = place("whi", [P, KCH // 2, COLS], f32r)
        wlo = place("wlo", [P, KCH // 2, COLS], f32r)
        buf = [place(f"buf{i}", [P, TILES, COLS], f32) for i in range(4)]
        gfin = place("gfin", [P, D], f32)
        kst = place("kst", [P, 2, S], f32)
        vst = place("vst", [P, 3, P], f32)
        half_qk = RET_QK // 2
        small = place("small", [P, SMALL], f32)
        ident = small[:, 0:P]
        rope = small[:, P:P + 2 * TILES * half_qk].rearrange("p (a t d) -> p a t d", a=2, t=TILES)
        gmix, gret, gffn, sink = [small[:, SMALL - (4 - i) * KCH:SMALL - (3 - i) * KCH] for i in range(4)]
        roper = place("roper", [P, 2, TILES, half_qk], f32)
        nsink = place("nsink", [P, 16], f32)
        ssq = place("ssq", [P, 2], f32)
        msq = place("msq", [P, 4], f32)
        rstd = place("rstd", [P, 2], f32)
        rstd_half = place("rstd_half", [P, 2], f32)
        ssq2 = place("ssq2", [P, TILES, GROUPS], f32)
        sum2 = place("sum2", [P, 2], f32)
        rstd2 = place("rstd2", [P, 2], f32)
        rstd3 = place("rstd3", [P, 2], f32)
        ssqr = place("ssqr", [P, 2, TILES], f32)
        powr = place("powr", [P, 2, TILES], f32)
        retsc = place("retsc", [P, 2, TILES], f32)
        mhalf = place("mhalf", [P, 4], f32)
        mx = place("mx", [P, 4], f32)
        negm = place("negm", [P, 4], f32)
        esd = place("esd", [P, 4], f32)
        es = place("es", [P, 4], f32)
        sums = place("sums", [P, 4], f32)
        den = place("den", [P, 4], f32)
        rden = place("rden", [P, 4], f32)
        assert here[0] <= nc.sbuf_usable_end, here[0]
        xin = place("xin", [P, TILES, D], f32, at_b)
        xt = place("xt", [P, KCH, S], f32, at_b + 16 * K)
        junk = place("junk", [P, D], f32, at_c + 24 * K)
        qkT = place("qkT", [P, 2 * RET_HEADS, S], f32, at_c)
        qbd = place("qbd", [P, 4, NCHUNK, P], f32, at_c + 16 * K)
        decay = place("decay", [P, RET_HEADS, RET_COLS], f32, at_c + 16 * K)
        ptr = place("ptr", [P, 2, RET_COLS], f32, at_c + 28 * K)
        final = place("final", [P, TILES, D], f32, at_c)
        kT = place("kT", [P, KV_HEADS, S], f32, at_m)
        vwin = place("vwin", [P, 3, KV_HEADS, P], f32, at_m + 4 * K)
        prob = place("prob", [P, 4, P], f32, at_m + 10 * K)
        probT = place("probT", [P, 4, P], f32, at_m + 12 * K)

        acc = [ctx.enter_context(nc.psum_tensor(f"acc{i}", [P, TILES, COLS], f32)) for i in range(2)]
        tps = ctx.enter_context(nc.psum_tensor("tps", [P, GCH, S], f32))
        sps = ctx.enter_context(nc.psum_tensor("sps", [P, 4, P], f32))
        pps = ctx.enter_context(nc.psum_tensor("pps", [P, 4, P], f32))
        flat = "p a b -> p (a b)"
        rs_ps = [sps[:].rearrange(flat), pps[:].rearrange(flat)]
        out_ps = tps[:].rearrange("p (i t) e -> p i t e", t=TILES)

        raw_full = [sem(f"raw_full{s}") for s in range(LOADS)]
        hi_ready, lo_ready, unit_done = sem("hi_ready"), sem("lo_ready"), sem("unit_done")
        evacuated = [sem("evacuated0"), sem("evacuated1")]
        xt_full = [sem(f"xt_full{u}") for u in range(UNITS)]
        first_full, x_full = sem("first_full"), sem("x_full")
        xt_gained, xt_hi = sem("xt_gained"), sem("xt_hi")
        warm = sem("warm")
        const_full, fin_full = sem("const_full"), sem("fin_full")
        decay_full = sem("decay_full")
        xres_full = [sem(f"xres_full{j}") for j in range(GROUPS)]
        t_full, t_free = sem("t_full"), sem("t_free")
        t_hi = sem("t_hi")
        hT_ready, retT_ready, h2T_ready = sem("hT_ready"), sem("retT_ready"), sem("h2T_ready")
        own = sem("own")
        mhalf_set, ssq_ready, ms_ready = sem("mhalf_set"), sem("ssq_ready"), sem("ms_ready")
        pow_ready, rstd_ready = sem("pow_ready"), sem("rstd_ready")
        consts_ready = sem("consts_ready")
        vshift, vst_ready, rope_ready = sem("vshift"), sem("vst_ready"), sem("rope_ready")
        s_full, negm_ready, exp_done, p_ready = sem("s_full"), sem("negm_ready"), sem("exp_done"), sem("p_ready")
        pt_full, pt_ready, av_full, att_hi, att_lo = sem("pt_full"), sem("pt_ready"), sem("av_full"), sem("att_hi"), sem("att_lo")
        kst_ready, rs_full, ptr_ready = sem("kst_ready"), sem("rs_full"), sem("ptr_ready")
        rssq_ready, rms_ready, rpow_ready, ret_ready = sem("rssq_ready"), sem("rms_ready"), sem("rpow_ready"), sem("ret_ready")
        rgate_ready, gated_ready = sem("rgate_ready"), sem("gated_ready")
        m_ready, u_ready = sem("m_ready"), sem("u_ready")
        x1_sq, ms2_ready, rstd2_ready = sem("x1_sq"), sem("ms2_ready"), sem("rstd2_ready")
        down_sq, ms3_ready, rstd3_ready = sem("down_sq"), sem("ms3_ready"), sem("rstd3_ready")
        final_g, final_act, final_dve, stored = sem("final_g"), sem("final_act"), sem("final_dve"), sem("stored")

        T_K = 0
        T_STAGE1 = T_K + 1
        T_STAGE3 = T_STAGE1 + 8
        T_STAGE4 = T_STAGE3 + 8
        T_STAGE5 = T_STAGE4 + 4
        T_STAGE6 = T_STAGE5 + 4
        B1, B2, B3, B4, B5, B6 = 1, 9, 17, 25, 33, 37

        turned = buf[1][:].rearrange("p t (m n) -> p (t m) n", n=S)

        def gained(u):
            return buf[2 + u % 2][:, 0, :].rearrange("p (k n) -> p k n", n=S)

        block = ctx.enter_context(nc.Block())

        @block.sync
        def _(sp):
            def load(B, src, s):
                src = src.rearrange("(k p) n -> p k n", p=P)
                sp.lower_ap_dma(src)
                if not B.very_first:
                    sp.wait_ge(lo_ready, B.number * UNITS + (2 * s + 2 - UNITS))
                sp.dma_start(raw[:, GCH * s:GCH * (s + 1), :],
                             src).then_inc(raw_full[s], 16)

            def load_block(B, w, col, row=0):
                for s in range(LOADS):
                    load(B, w[ds(row + s * 512, 512), ds(col, COLS)], s)

            def load_xt(u):
                ch = slice(u * UCH, (u + 1) * UCH)
                sp.dma_start(xt[:, ch, :], x_t[:, ch, :]).then_inc(xt_full[u], 16)

            load_xt(0)
            w = w_in[0:COLS, OFF_AKV:OFF_AKV + COLS].rearrange("(k p) n -> p k n", p=P)
            sp.dma_start(raw[:, 0:UCH, :], w[:, 0:UCH, :]).then_inc(first_full, 16)
            load_xt(1)
            sp.dma_start(raw[:, UCH:GCH, :], w[:, UCH:GCH, :]).then_inc(raw_full[0], 16)
            for s in range(1, LOADS):
                load_xt(2 * s)
                load(Block(0), w_in[s * 512:(s + 1) * 512, OFF_AKV:OFF_AKV + COLS], s)
                load_xt(2 * s + 1)
            for s in range(2):
                load(Block(1), w_in[s * 512:(s + 1) * 512, OFF_AQ:OFF_AQ + COLS], s)
            sp.dma_start(xin[:], x.rearrange("(t p) n -> p t n", p=P)).then_inc(x_full, 16)
            for s in range(2, LOADS):
                load(Block(1), w_in[s * 512:(s + 1) * 512, OFF_AQ:OFF_AQ + COLS], s)
            load_block(Block(2), w_in, OFF_RQK)

            def stage1(j):
                load_block(Block(B1, 2, j), w_in, j * COLS + OFF_AQ)
                load_block(Block(B1 + 1, 2, j), w_in, j * COLS + OFF_RQK)

            def stage2(j):
                load_block(Block(B2, 2, j), w_gate, j * COLS + D)
                load_block(Block(B2 + 1, 2, j), w_att, j * COLS)

            def stage3(j):
                load_block(Block(B3, 2, j), w_in, j * COLS + OFF_RV)
                load_block(Block(B3 + 1, 2, j), w_in, j * COLS + OFF_RG)

            def stage4(j):
                load_block(Block(B4, 2, j), w_gate, j * COLS)
                load_block(Block(B4 + 1, 2, j), w_ret, j * COLS)

            with sp.Fori(1, 4) as j:
                stage1(j)
            stage2(0)
            with sp.Fori(1, 4) as j:
                stage2(j)
            sp.wait_ge(s_full, 16)
            sp.dma_start(decay[:], decay_c).then_inc(decay_full, 16)
            stage3(0)
            with sp.Fori(1, 4) as j:
                stage3(j)
            sp.dma_start(gfin[:], g_fin.partition_broadcast(P)).then_inc(fin_full, 16)
            stage4(0)
            with sp.Fori(1, 4) as j:
                stage4(j)
            for j in range(GROUPS):
                if j == GROUPS - 1:
                    load_block(Block(B5), w_out, 0)
                sp.wait_ge(m_ready, j + 1)
                sp.dma_start(mix[:, :, j * COLS:(j + 1) * COLS],
                             x[:, j * COLS:(j + 1) * COLS].rearrange("(t p) n -> p t n", p=P)).then_inc(xres_full[j], 16)
            for j in range(1, GROUPS):
                load_block(Block(B5 + j), w_out, j * COLS)

            def stage6(q):
                for i in range(4):
                    load_block(Block(B6 + i, 8, q), w_up, q * D + i * COLS)
                for i in range(4):
                    load_block(Block(B6 + 4 + i, 8, q), w_down, i * COLS, q * D)

            stage6(0)
            with sp.Fori(1, 4) as q:
                stage6(q)
            for t, ready in ((0, final_act), (1, final_dve)):
                for h in range(2):
                    sp.wait_ge(ready, h + 1)
                    sp.dma_start(out[t * P:(t + 1) * P, h * 1024:(h + 1) * 1024],
                                 final[:, t, h * 1024:(h + 1) * 1024]).then_inc(stored, 16)
            sp.wait_ge(stored, 64)

        @block.tensor
        def _(pe):
            def gemm(B, hi, lo, u0, u1):
                for u in range(u0, u1):
                    if u == 0 and B.reused:
                        pe.wait_ge(evacuated[B.parity], B.turn)
                    pe.wait_ge(lo_ready, B.unit(u))
                    for kk in range(UCH):
                        k, slot = u * UCH + kk, (u * UCH + kk) % (KCH // 2)
                        for t in range(TILES):
                            tok = slice(t * P, (t + 1) * P)
                            for n, (a, b) in enumerate(((hi, whi), (hi, wlo), (lo, whi))):
                                last = nc.tensor.matmul(acc[B.parity][:, t, :], a[:, k, tok], b[:, slot, :],
                                                        start=(k == 0 and n == 0), stop=(k == KCH - 1 and n == 2))
                    last.then_inc(unit_done, 1)

            def transposes(turn, src):
                if later(turn):
                    pe.wait_ge(t_free, turn)
                for m in range(GCH):
                    for t in range(TILES):
                        last = nc.tensor.transpose(tps[:, m, t * P:(t + 1) * P], src(t, m), ident)
                last.then_inc(t_full, 1)

            def from_buf(b):
                return lambda t, m: b[:, t, m * P:(m + 1) * P]

            def scores(g, c):
                n = g * NCHUNK + c
                if c == 0:
                    pe.wait_ge(t_free, g * 2 + (T_STAGE1 + 1))
                if later(n):
                    pe.wait_ge(exp_done, n)
                k0, kn, _ = KEYS[c]
                for pair in range(4):
                    last = nc.tensor.matmul(sps[:, pair, 0:kn], qbd[:, pair, c, :],
                                            kT[:, ds(g, 1), k0:k0 + kn].rearrange("p a n -> p (a n)"),
                                            start=True, stop=True)
                last.then_inc(s_full, 1)

            def prob_transposes(g, c):
                n = g * NCHUNK + c
                pe.wait_ge(p_ready, n + 1)
                if later(n):
                    pe.wait_ge(att_lo, n)
                for pair in range(4):
                    last = nc.tensor.transpose(pps[:, pair, :], prob[:, pair, :], ident)
                last.then_inc(pt_full, 1)

            def attend(g, c):
                if c == 0:
                    pe.wait_ge(vst_ready, g + 1)
                pe.wait_ge(pt_ready, g * NCHUNK + c + 1)
                nc.tensor.matmul(pps[:].rearrange(flat), vst[:, KEYS[c][2], :], probT[:].rearrange(flat),
                                 start=True, stop=True).then_inc(av_full, 1)

            pe.wait_ge(warm, 1)
            for _ in range(WARM_UP):
                nc.tensor.matmul(pps[:, 0, :], mix[:, 0, 0:P], mix[:, 0, 0:P], start=True, stop=True)
            for u in range(UNITS):
                pe.wait_ge(hT_ready, u + 1)
                gemm(Block(0), ta_hi, ta_lo, u, u + 1)

            def tail_a(g, B, hi, lo):
                gemm(B, hi, lo, 0, 1)
                attend(g, 0)
                gemm(B, hi, lo, 1, 4)
                prob_transposes(g, 1)
                scores(g, 2)
                gemm(B, hi, lo, 4, 5)
                attend(g, 1)
                pe.wait_ge(rope_ready, g + 1)
                transposes(g * 2 + T_STAGE1 + 1, from_buf(buf[1]))
                gemm(B, hi, lo, 5, 7)
                prob_transposes(g, 2)
                scores(g, 3)
                gemm(B, hi, lo, 7, 8)
                attend(g, 2)

            def stage1(j, first):
                A, R = Block(B1, 2, j), Block(B1 + 1, 2, j)
                if first:
                    gemm(A, ta_hi, ta_lo, 0, 6)
                    pe.wait_ge(const_full, 16)
                    pe.wait_ge(evacuated[0], 1)
                    transposes(T_K, from_buf(buf[1]))
                    gemm(A, ta_hi, ta_lo, 6, 8)
                else:
                    tail_a(j - 1, A, ta_hi, ta_lo)
                gemm(R, ta_hi, ta_lo, 0, 2)
                pe.wait_ge(evacuated[1], A.turn + 1)
                transposes(j * 2 + T_STAGE1, from_buf(buf[0]))
                gemm(R, ta_hi, ta_lo, 2, 3)
                if not first:
                    prob_transposes(j - 1, 3)
                gemm(R, ta_hi, ta_lo, 3, 4)
                if not first:
                    attend(j - 1, 3)
                scores(j, 0)
                gemm(R, ta_hi, ta_lo, 4, 8)
                prob_transposes(j, 0)
                scores(j, 1)

            stage1(0, True)
            with pe.Fori(1, 4) as j:
                stage1(j, False)

            tail_a(3, Block(B2), ta_hi, ta_lo)
            gemm(Block(B2 + 1), tb_hi, tb_lo, 0, 3)
            prob_transposes(3, 3)
            gemm(Block(B2 + 1), tb_hi, tb_lo, 3, 4)
            attend(3, 3)
            gemm(Block(B2 + 1), tb_hi, tb_lo, 4, 6)
            pe.wait_ge(att_lo, 16)
            gemm(Block(B2 + 1), tb_hi, tb_lo, 6, 8)
            with pe.Fori(1, 4) as j:
                gemm(Block(B2, 2, j), ta_hi, ta_lo, 0, 8)
                gemm(Block(B2 + 1, 2, j), tb_hi, tb_lo, 0, 8)

            def stage3(j, first):
                V, G = Block(B3, 2, j), Block(B3 + 1, 2, j)
                gemm(V, ta_hi, ta_lo, 0, 4)
                if not first:
                    pe.wait_ge(gated_ready, j)
                    transposes(j * 2 + T_STAGE3 - 1, from_buf(buf[3]))
                gemm(V, ta_hi, ta_lo, 4, 8)
                gemm(G, ta_hi, ta_lo, 0, 2)
                pe.wait_ge(kst_ready, j + 1)
                if not first:
                    pe.wait_ge(ptr_ready, j * 2)
                for i in range(2):
                    q = qkT[:, ds(j * 2 + i, 1), :].rearrange("p a n -> p (a n)")
                    nc.tensor.matmul(rs_ps[i][:, 0:S], kst[:, i, 0:P], q, start=True, stop=True)
                    nc.tensor.matmul(rs_ps[i][:, S:RET_COLS], kst[:, i, P:S],
                                     qkT[:, ds(j * 2 + i, 1), P:S].rearrange("p a n -> p (a n)"),
                                     start=True, stop=True).then_inc(rs_full, 1)
                gemm(G, ta_hi, ta_lo, 2, 5)
                pe.wait_ge(evacuated[1], V.turn + 1)
                pe.wait_ge(ptr_ready, j * 2 + 2)
                pe.wait_ge(t_free, j * 2 + T_STAGE3)
                for i in range(2):
                    v = [buf[0][:, t, i * RET_V:(i + 1) * RET_V] for t in range(TILES)]
                    nc.tensor.matmul(out_ps[:, i, 0, :], ptr[:, i, 0:P], v[0], start=True, stop=True)
                    nc.tensor.matmul(out_ps[:, i, 1, :], ptr[:, i, P:S], v[0], start=True, stop=False)
                    last = nc.tensor.matmul(out_ps[:, i, 1, :], ptr[:, i, S:RET_COLS], v[1], start=False, stop=True)
                last.then_inc(t_full, 1)
                gemm(G, ta_hi, ta_lo, 5, 8)

            stage3(0, True)
            with pe.Fori(1, 4) as j:
                stage3(j, False)

            def stage4(j, first):
                gemm(Block(B4, 2, j), ta_hi, ta_lo, 0, 3)
                if first:
                    pe.wait_ge(gated_ready, 4)
                    transposes(T_STAGE3 + 7, from_buf(buf[3]))
                gemm(Block(B4, 2, j), ta_hi, ta_lo, 3, 8)
                if first:
                    pe.wait_ge(retT_ready, 4)
                gemm(Block(B4 + 1, 2, j), tb_hi, tb_lo, 0, 8)

            stage4(0, True)
            with pe.Fori(1, 4) as j:
                stage4(j, False)

            for j in range(GROUPS):
                if j == 0:
                    pe.wait_ge(t_free, T_STAGE4 + 3)
                gemm(Block(B5 + j), tc_hi, tc_lo, 0, 6)
                if j == 0:
                    pe.wait_ge(t_free, T_STAGE4 + 4)
                gemm(Block(B5 + j), tc_hi, tc_lo, 6, 8)

            def stage6(q, first):
                B = [Block(B6 + i, 8, q) for i in range(8)]
                if first:
                    pe.wait_ge(h2T_ready, 3)
                    gemm(B[0], ta_hi, ta_lo, 0, 6)
                    pe.wait_ge(h2T_ready, 4)
                    gemm(B[0], ta_hi, ta_lo, 6, 8)
                else:
                    gemm(B[0], ta_hi, ta_lo, 0, 8)
                for i in range(1, 5):
                    hi, lo = (ta_hi, ta_lo) if i < 4 else (tb_hi, tb_lo)
                    if i == 4:
                        pe.wait_ge(t_free, q * 4 + (T_STAGE6 + 3))
                    gemm(B[i], hi, lo, 0, 6)
                    if i == 4:
                        pe.wait_ge(t_free, q * 4 + (T_STAGE6 + 4))
                    gemm(B[i], hi, lo, 6, 8)
                for i in range(5, 8):
                    gemm(B[i], tb_hi, tb_lo, 0, 8)

            stage6(0, True)
            with pe.Fori(1, 4) as q:
                stage6(q, False)

        @block.scalar
        def _(act):
            def split(B, u0, u1):
                for u in range(u0, u1):
                    if B.very_first and u == 0:
                        act.wait_ge(first_full, 16)
                    elif u % 2 == 0 or (B.very_first and u == 1):
                        act.wait_ge(raw_full[u // 2], B.number * 16 + 16)
                    if not B.very_first or u >= 4:
                        act.wait_ge(unit_done, B.unit(u - 4))
                    s = u * UCH % (KCH // 2)
                    nc.scalar.activation(whi[:, s:s + UCH, :], raw[:, u * UCH:(u + 1) * UCH, :],
                                         ACT.Copy).then_inc(hi_ready, 1)

            def scaled(B, dst, func, scale):
                act.wait_ge(unit_done, B.unit(UNITS - 1))
                for t in range(TILES):
                    last = nc.scalar.activation(dst[:, t, :], acc[B.parity][:, t, :], func, scale=scale[:, t:t + 1])
                return last

            def hi_from_turned(turn, dst, g):
                act.wait_ge(t_full, turn + 1)
                nc.scalar.activation(dst[:, ds(g * GCH, GCH), :], turned, ACT.Copy).then_inc(t_hi, 1)

            def hi_from_gained(turn, src, dst, g):
                act.wait_ge(t_free, turn + 1)
                nc.scalar.activation(dst[:, ds(g * GCH, GCH), :], src[:].rearrange("p t (k n) -> p (t k) n", n=S),
                                     ACT.Copy).then_inc(t_hi, 1)

            def exps(g, c):
                n = g * NCHUNK + c
                kn = KEYS[c][1]
                act.wait_ge(negm_ready, n + 1)
                if later(n):
                    act.wait_ge(pt_full, n)
                for pair in range(4):
                    nc.scalar.activation(prob[:, pair, 0:kn], sps[:, pair, 0:kn], ACT.Exp, scale=ATT_SCALE,
                                         bias=negm[:, pair:pair + 1], accum_out=sums[:, pair:pair + 1])
                nc.scalar.activation(es[:], esd[:], ACT.Exp).then_inc(exp_done, 1)

            def probs_out(g, c):
                n = g * NCHUNK + c
                act.wait_ge(pt_full, n + 1)
                if later(n):
                    act.wait_ge(av_full, n)
                nc.scalar.activation(probT[:], pps[:], ACT.Copy).then_inc(pt_ready, 1)

            def attended_hi(g, c):
                act.wait_ge(av_full, g * NCHUNK + c + 1)
                v = pps[:].rearrange("p a (h q) -> p a h q", h=2)
                for h in range(2):
                    part = slice(h * 64, h * 64 + 64)
                    last = nc.scalar.activation(tb_hi[part, ds(g * GCH, GCH), c * CHUNK:(c + 1) * CHUNK],
                                                v[part, :, h, :], ACT.Copy)
                last.then_inc(att_hi, 1)

            act.dma_start(small[:], small_c).then_inc(const_full, 16)

            B = Block(0)
            for u in range(UNITS):
                if u % 2:
                    split(B, u, u + 1)
                act.wait_ge(xt_gained, u + 1)
                nc.scalar.activation(ta_hi[:, u * UCH:(u + 1) * UCH, :], gained(u), ACT.Copy).then_inc(xt_hi, 1)
                if u % 2 == 0:
                    split(B, u, u + 1)

            def tail_a(g, B):
                split(B, 0, 1)
                exps(g, 0)
                split(B, 1, 4)
                probs_out(g, 0)
                split(B, 4, 5)
                exps(g, 1)
                attended_hi(g, 0)
                split(B, 5, 8)
                probs_out(g, 1)

            def tail_r(g, B):
                split(B, 0, 1)
                exps(g, 2)
                attended_hi(g, 1)
                split(B, 1, 3)
                probs_out(g, 2)
                split(B, 3, 4)
                exps(g, 3)
                attended_hi(g, 2)

            def stage1(j, first):
                A, R = Block(B1, 2, j), Block(B1 + 1, 2, j)
                if first:
                    split(A, 0, 4)
                    act.wait_ge(x_full, 16)
                    for t in range(TILES):
                        if t:
                            act.wait_ge(ssq_ready, t)
                        nc.scalar.activation(junk[:], xin[:, t, :], ACT.Square, accum_out=ssq[:, t:t + 1]).then_inc(ssq_ready, 1)
                        split(A, 4 + t, 5 + t)
                    act.wait_ge(rstd_ready, 1)
                    act.wait_ge(unit_done, Block(0).unit(UNITS - 1))
                    kd = buf[1][:].rearrange("p t (g e d) -> p t g e d", e=2, d=ATT_D)
                    vd = vwin[:].rearrange("p w g (e d) -> p w g e d", e=2)
                    for t in range(TILES):
                        kv = acc[0][:, t, :].rearrange("p (s g d) -> p s g d", s=2, d=ATT_D)
                        for e in range(2):
                            nc.scalar.activation(kd[:, t, :, e, :], kv[:, 0], ACT.Copy, scale=rstd[:, t:t + 1])
                            last = nc.scalar.activation(vd[:, 2 * t, :, e, :], kv[:, 1], ACT.Copy, scale=rstd[:, t:t + 1])
                    last.then_inc(evacuated[0], 1)
                    split(A, 6, 8)
                    split(R, 0, 1)
                    act.wait_ge(t_full, T_K + 1)
                    nc.scalar.activation(kT[:], tps[:], ACT.Copy).then_inc(t_free, 1)
                    split(R, 1, 4)
                else:
                    tail_a(j - 1, A)
                    tail_r(j - 1, R)
                    act.wait_ge(t_full, j * 2 + (T_STAGE1 - 1))
                scaled(A, buf[0], ACT.Copy, rstd).then_inc(evacuated[1], 1)
                split(R, 4, 6)
                act.wait_ge(t_full, j * 2 + (T_STAGE1 + 1))
                act.wait_ge(consts_ready, 1)
                for h in range(2):
                    part = slice(h * 64, h * 64 + 64)
                    last = nc.scalar.activation(qbd[part, :, :, part], tps[part, :, :].rearrange("p a (c q) -> p a c q", q=CHUNK),
                                                ACT.Copy)
                last.then_inc(t_free, 1)
                split(R, 6, 7)
                if not first:
                    probs_out(j - 1, 3)
                split(R, 7, 8)
                if not first:
                    attended_hi(j - 1, 3)

            stage1(0, True)
            with act.Fori(1, 4) as j:
                stage1(j, False)

            tail_a(3, Block(B2))
            tail_r(3, Block(B2 + 1))
            act.wait_ge(rope_ready, 4)
            scaled(Block(B2), buf[2], ACT.Tanh, rstd_half).then_inc(evacuated[1], 1)
            split(Block(B2 + 1), 4, 7)
            probs_out(3, 3)
            split(Block(B2 + 1), 7, 8)
            attended_hi(3, 3)
            with act.Fori(1, 4) as j:
                G, A = Block(B2, 2, j), Block(B2 + 1, 2, j)
                split(G, 0, 8)
                split(A, 0, 4)
                act.wait_ge(evacuated[0], A.turn)
                scaled(G, buf[2], ACT.Tanh, rstd_half).then_inc(evacuated[1], 1)
                split(A, 4, 8)

            def retention_squares(j, B):
                act.wait_ge(t_full, j * 2 + (T_STAGE3 + 1))
                if later(j):
                    act.wait_ge(rms_ready, j)
                for i in range(2):
                    for t in range(TILES):
                        last = nc.scalar.activation(junk3[:, i, t, :], out_ps[:, i, t, :], ACT.Square,
                                                    accum_out=ssqr[:, i, t:t + 1])
                last.then_inc(rssq_ready, 1)

            junk3 = buf[3][:].rearrange("p t (i e) -> p i t e", i=2)

            def tail3(j, B):
                split(B, 0, 1)
                if later(j):
                    act.wait_ge(t_full, j * 2 + T_STAGE3)
                retention_squares(j, B)
                split(B, 1, 4)
                if later(j):
                    act.wait_ge(retT_ready, j)
                else:
                    act.wait_ge(evacuated[0], Block(B3 - 1).turn + 1)
                scaled(Block(B3 + 1, 2, j), buf[2], ACT.Tanh, rstd_half).then_inc(rgate_ready, 1)
                split(B, 4, 8)
                hi_from_gained(j * 2 + (T_STAGE3 + 1), buf[2], tb_hi, j)

            def stage3(j, first):
                V, G = Block(B3, 2, j), Block(B3 + 1, 2, j)
                if first:
                    split(V, 0, 8)
                    act.wait_ge(t_free, T_STAGE1 + 8)
                else:
                    tail3(j - 1, V)
                    act.wait_ge(rs_full, j * 2)
                nc.scalar.activation(kst[:], qkT[:, ds(j * 2 + RET_HEADS, 2), :], ACT.Copy).then_inc(kst_ready, 1)
                split(G, 0, 4)
                if not first:
                    act.wait_ge(t_full, j * 2 + (T_STAGE3 - 1))
                scaled(V, buf[0], ACT.Copy, rstd).then_inc(evacuated[1], 1)
                split(G, 4, 8)

            stage3(0, True)
            with act.Fori(1, 4) as j:
                stage3(j, False)

            def stage4(j, first):
                G, R = Block(B4, 2, j), Block(B4 + 1, 2, j)
                if first:
                    tail3(3, G)
                else:
                    split(G, 0, 8)
                    hi_from_turned(j + (T_STAGE4 - 1), tc_hi, j - 1)
                split(R, 0, 4)
                if first:
                    act.wait_ge(retT_ready, 4)
                else:
                    act.wait_ge(evacuated[0], R.turn)
                scaled(G, buf[2], ACT.Tanh, rstd_half).then_inc(evacuated[1], 1)
                split(R, 4, 8)

            stage4(0, True)
            with act.Fori(1, 4) as j:
                stage4(j, False)

            def residual_squares(B, j, done):
                act.wait_ge(evacuated[B.parity], B.turn + 1)
                for t in range(TILES):
                    last = nc.scalar.activation(buf[3][:, t, :], mix[:, t, j * COLS:(j + 1) * COLS], ACT.Square,
                                                accum_out=ssq2[:, t, j:j + 1])
                last.then_inc(done, 1)

            for j in range(GROUPS + 1):
                B = Block(B5 + j)
                split(B, 0, 5)
                if j:
                    if j == 1:
                        act.wait_ge(t_full, T_STAGE4 + 4)
                    residual_squares(Block(B5 + j - 1), j - 1, x1_sq)
                split(B, 5, 8)
                if j == 0:
                    hi_from_turned(T_STAGE4 + 3, tc_hi, 3)
                else:
                    hi_from_gained(T_STAGE5 + j - 1, buf[2], ta_hi, j - 1)

            def stage6(q, first):
                B = [Block(B6 + i, 8, q) for i in range(8)]
                if not first:
                    split(B[0], 0, 5)
                    residual_squares(Block(B6 - 1, 8, q), 3, down_sq)
                    split(B[0], 5, 8)
                for i in range(1, 5):
                    split(B[i], 0, 4)
                    if first and i == 1:
                        act.wait_ge(rstd2_ready, 1)
                    else:
                        act.wait_ge(t_full, q * 4 + (T_STAGE6 + i - 1))
                    scaled_relu(B[i - 1])
                    split(B[i], 4, 8)
                    hi_from_turned(q * 4 + (T_STAGE6 + i - 1), tb_hi, i - 1)
                for i in range(5, 8):
                    split(B[i], 0, 5)
                    residual_squares(B[i - 1], i - 5, down_sq)
                    split(B[i], 5, 8)

            def scaled_relu(B):
                scaled(B, buf[0], ACT.Relu, rstd2).then_inc(evacuated[B.parity], 1)

            stage6(0, True)
            with act.Fori(1, 4) as q:
                stage6(q, False)
            residual_squares(Block(68), 3, down_sq)
            act.wait_ge(rstd3_ready, 1)
            act.wait_ge(final_g, 2)
            for h in range(2):
                cols = slice(h * 1024, (h + 1) * 1024)
                nc.scalar.activation(final[:, 0, cols], final[:, 0, cols], ACT.Copy, scale=rstd3[:, 0:1]).then_inc(final_act, 1)

        @block.vector
        def _(dve):
            V_ = nc.vector
            mine = Steps(own)

            def split(B, u0, u1):
                for u in range(u0, u1):
                    dve.wait_ge(hi_ready, B.unit(u))
                    s = u * UCH % (KCH // 2)
                    V_.tensor_tensor(wlo[:, s:s + UCH, :], raw[:, u * UCH:(u + 1) * UCH, :],
                                     whi[:, s:s + UCH, :].bitcast(f32), ALU.subtract).then_inc(lo_ready, 1)

            def split_and_turn(B, u0, u1, turn, src, ready, n):
                src = src.rearrange("p t (m f) -> p m t f", f=P)
                dst = turned.rearrange("p m (t n) -> p m t n", n=P)
                dve.wait_ge(ready, n)
                dve.wait_ge(t_free, turn)
                pieces = [(i, o) for i in range(0, P, SQ) for o in range(0, P, SQ)]
                for u in range(u0, u1):
                    share = len(pieces) * (u - u0) // (u1 - u0), len(pieces) * (u - u0 + 1) // (u1 - u0)
                    for i, o in pieces[share[0]:share[1]]:
                        last = V_.transpose(dst[o:o + SQ, :, :, i:i + SQ], src[i:i + SQ, :, :, o:o + SQ])
                    if u == u1 - 1:
                        last.then_inc(t_full, 1)
                    split(B, u, u + 1)

            def gain(turn, dst, gains, g):
                dve.wait_ge(t_full, turn + 1)
                gsl = gains[:, ds(g * GCH, GCH)].unsqueeze(2).to_broadcast([P, GCH, S])
                V_.tensor_tensor(dst[:].rearrange("p t (k n) -> p (t k) n", n=S), turned, gsl, ALU.mult).then_inc(t_free, 1)

            def lo_from_gained(n, src, hi, lo, g, done):
                dve.wait_ge(t_hi, n)
                V_.tensor_tensor(lo[:, ds(g * GCH, GCH), :], src[:].rearrange("p t (k n) -> p (t k) n", n=S),
                                 hi[:, ds(g * GCH, GCH), :].bitcast(f32), ALU.subtract).then_inc(done, 1)

            def lo_from_turned(n, hi, lo, g):
                dve.wait_ge(t_hi, n)
                V_.tensor_tensor(lo[:, ds(g * GCH, GCH), :], turned, hi[:, ds(g * GCH, GCH), :].bitcast(f32),
                                 ALU.subtract).then_inc(t_free, 1)

            V_.memset(mix[:, 0, 0:P], 0.0).then_inc(warm, 1)
            V_.memset(qbd[:], 0.0).then_inc(consts_ready, 1)
            dve.wait_ge(const_full, 16)
            B = Block(0)

            def gain_xt(u):
                ch = slice(u * UCH, (u + 1) * UCH)
                dve.wait_ge(xt_full[u], 16)
                if u >= 2:
                    dve.wait_ge(hT_ready, u - 1)
                V_.tensor_tensor(gained(u), xt[:, ch, :], gmix[:, ch].unsqueeze(2).to_broadcast([P, UCH, S]),
                                 ALU.mult).then_inc(xt_gained, 1)

            gain_xt(0)
            for u in range(UNITS):
                ch = slice(u * UCH, (u + 1) * UCH)
                if u % 2:
                    split(B, u, u + 1)
                if 0 < u < UNITS - 1:
                    gain_xt(u + 1)
                dve.wait_ge(xt_hi, u + 1)
                V_.tensor_tensor(ta_lo[:, ch, :], gained(u), ta_hi[:, ch, :].bitcast(f32), ALU.subtract).then_inc(hT_ready, 1)
                if u % 2 == 0:
                    split(B, u, u + 1)
                if u == 0:
                    gain_xt(1)
            mine.step(V_.tensor_scalar(nsink[:], sink, -1.0, None, ALU.mult))

            def maxima(g, c):
                n = g * NCHUNK + c
                dve.wait_ge(s_full, n + 1)
                if later(n):
                    dve.wait_ge(exp_done, n)
                mine.step(V_.tensor_reduce(mx[:], sps[:, :, 0:KEYS[c][1]], AX.X, ALU.max))
                mine.wait(dve)
                mine.step(V_.scalar_tensor_tensor(negm[:], mx[:], -ATT_SCALE, nsink[:, ds(g * 4, 4)], ALU.mult, ALU.min))
                mine.wait(dve)
                V_.tensor_tensor(esd[:], negm[:], nsink[:, ds(g * 4, 4)], ALU.subtract).then_inc(negm_ready, 1)

            def normalise(g, c):
                n = g * NCHUNK + c
                kn = KEYS[c][1]
                dve.wait_ge(exp_done, n + 1)
                mine.step(V_.tensor_tensor(den[:], sums[:], es[:], ALU.add))
                mine.wait(dve)
                mine.step(V_.reciprocal(rden[:], den[:]))
                if c == 0:
                    mine.step(V_.memset(prob[:, :, kn:P], 0.0))
                mine.wait(dve)
                V_.tensor_tensor(prob[:, :, 0:kn], prob[:, :, 0:kn], rden[:].unsqueeze(2).to_broadcast([P, 4, kn]),
                                 ALU.mult).then_inc(p_ready, 1)

            def attended_lo(g, c):
                dve.wait_ge(att_hi, g * NCHUNK + c + 1)
                v = pps[:].rearrange("p a (h q) -> p a h q", h=2)
                for h in range(2):
                    part = slice(h * 64, h * 64 + 64)
                    at = (part, ds(g * GCH, GCH), slice(c * CHUNK, (c + 1) * CHUNK))
                    last = V_.tensor_tensor(tb_lo[at], v[part, :, h, :], tb_hi[at].bitcast(f32), ALU.subtract)
                last.then_inc(att_lo, 1)

            def rotate(g, B):
                dve.wait_ge(unit_done, B.unit(UNITS - 1))
                half = RET_QK // 2
                v = acc[B.parity][:].rearrange("p t (h x d) -> p t h x d", x=2, d=half)
                cos = roper[:, 0].unsqueeze(2).to_broadcast([P, TILES, 4, half])
                sin = roper[:, 1].unsqueeze(2).to_broadcast([P, TILES, 4, half])
                o = buf[1][:].rearrange("p t (h x d) -> p t h x d", x=2, d=half)
                tmp = [b[:].rearrange("p t (h d) -> p t h d", d=half)[:, :, 4 * i:4 * i + 4, :]
                       for b in (buf[2], buf[3]) for i in range(2)]
                V_.tensor_tensor(tmp[0], v[:, :, :, 0, :], cos, ALU.mult)
                V_.tensor_tensor(tmp[1], v[:, :, :, 1, :], sin, ALU.mult)
                mine.step(V_.tensor_tensor(tmp[2], v[:, :, :, 1, :], cos, ALU.mult))
                V_.tensor_tensor(tmp[3], v[:, :, :, 0, :], sin, ALU.mult).then_inc(evacuated[B.parity], 1)
                dve.wait_ge(t_full, g * 2 + T_STAGE1)
                dve.wait_ge(evacuated[B.parity], B.turn + 1)
                V_.tensor_tensor(o[:, :, :, 0, :], tmp[0], tmp[1], ALU.subtract)
                V_.tensor_tensor(o[:, :, :, 1, :], tmp[2], tmp[3], ALU.add).then_inc(rope_ready, 1)

            def tail_a(g, B, R):
                split(B, 0, 2)
                normalise(g, 0)
                split(B, 2, 4)
                maxima(g, 1)
                rotate(g, R)
                split(B, 4, 6)
                normalise(g, 1)
                attended_lo(g, 0)
                split(B, 6, 8)
                maxima(g, 2)

            def tail_r(g, B):
                split(B, 0, 1)
                dve.wait_ge(t_full, g * 2 + (T_STAGE1 + 2))
                V_.tensor_copy(qkT[:, ds(g * 4, 4), :], tps[:]).then_inc(t_free, 1)
                normalise(g, 2)
                attended_lo(g, 1)
                split(B, 1, 3)
                maxima(g, 3)
                split(B, 3, 5)
                normalise(g, 3)
                attended_lo(g, 2)

            def stage1(j, first):
                A, R = Block(B1, 2, j), Block(B1 + 1, 2, j)
                if first:
                    split(A, 0, 5)
                    dve.wait_ge(ssq_ready, 2)
                    V_.tensor_scalar(msq[:, 0:2], ssq[:], 1.0 / D, EPS, ALU.mult, ALU.add).then_inc(ms_ready, 1)
                    dve.wait_ge(pow_ready, 1)
                    V_.tensor_scalar(rstd_half[:], rstd[:], 0.5, None, ALU.mult).then_inc(rstd_ready, 1)
                    split(A, 5, 6)
                    mine.step(V_.tensor_tensor(roper[:], rope,
                                               rstd[:].unsqueeze(1).unsqueeze(3).to_broadcast([P, 2, TILES, RET_QK // 2]), ALU.mult))
                    dve.wait_ge(evacuated[0], 1)
                    V_.tensor_copy(vwin[0:64, 1], vwin[64:128, 0])
                    V_.tensor_copy(vwin[64:128, 1], vwin[0:64, 2]).then_inc(vshift, 1)
                    split(A, 6, 8)
                    split(R, 0, 5)
                else:
                    tail_a(j - 1, A, Block(B1 + 1, 2, j - 1))
                    tail_r(j - 1, R)
                split(R, 5, 8)
                if not first:
                    attended_lo(j - 1, 3)
                maxima(j, 0)

            stage1(0, True)
            mine_at = OWN_STAGE1
            with dve.Fori(1, 4) as j:
                mine.enter_loop(j, 1, mine_at)
                stage1(j, False)
            mine.leave_loop(3, mine_at)

            def gate(B):
                dve.wait_ge(evacuated[1], B.turn + 1)
                mine.step(V_.tensor_scalar(buf[2][:], buf[2][:], 0.5, 0.5, ALU.mult, ALU.add))

            def gated_attention(j):
                B = Block(B2 + 1, 2, j)
                dve.wait_ge(unit_done, B.unit(UNITS - 1))
                mine.wait(dve)
                V_.tensor_tensor(mix[:, :, ds(j * COLS, COLS)], buf[2][:], acc[0][:], ALU.mult).then_inc(evacuated[0], 1)

            tail_a(3, Block(B2), Block(B2 - 1))
            tail_r(3, Block(B2 + 1))
            gate(Block(B2))
            split(Block(B2 + 1), 5, 8)
            attended_lo(3, 3)
            with dve.Fori(1, 4) as j:
                mine.enter_loop(j, 1, OWN_STAGE2)
                split(Block(B2, 2, j), 0, 4)
                gated_attention(j - 1)
                split(Block(B2, 2, j), 4, 8)
                split(Block(B2 + 1, 2, j), 0, 5)
                gate(Block(B2, 2, j))
                split(Block(B2 + 1, 2, j), 5, 8)
            mine.leave_loop(3, OWN_STAGE2)

            def tail3(j, B):
                split(B, 0, 2)
                dve.wait_ge(rssq_ready, j + 1)
                V_.tensor_scalar(msq[:], ssqr[:].rearrange("p i t -> p (i t)"), 1.0 / RET_V, EPS, ALU.mult, ALU.add).then_inc(rms_ready, 1)
                split(B, 2, 3)
                dve.wait_ge(rpow_ready, j + 1)
                mine.step(V_.tensor_tensor(retsc[:], powr[:], rstd_half[:].unsqueeze(1).to_broadcast([P, 2, TILES]), ALU.mult))
                mine.wait(dve)
                V_.tensor_tensor(buf[1][:].rearrange("p t (i e) -> p i t e", i=2), out_ps,
                                 retsc[:].unsqueeze(3).to_broadcast([P, 2, TILES, RET_V]), ALU.mult).then_inc(t_free, 1)
                split(B, 3, 4)
                dve.wait_ge(rgate_ready, j + 1)
                dve.wait_ge(t_free, j * 2 + (T_STAGE3 + 1))
                V_.tensor_tensor(buf[3][:], buf[1][:], acc[0][:], ALU.mult).then_inc(evacuated[0], 1)
                dve.wait_ge(evacuated[0], Block(B3 + 1, 2, j).turn + 1)
                V_.scalar_tensor_tensor(buf[3][:].rearrange(flat), buf[2][:].rearrange(flat), 1.0,
                                        buf[3][:].rearrange(flat), ALU.add, ALU.mult).then_inc(gated_ready, 1)
                split(B, 4, 8)
                dve.wait_ge(gated_ready, j + 1)
                gain3(j)

            def gain3(j):
                dve.wait_ge(t_full, j * 2 + (T_STAGE3 + 2))
                gsl = gret[:, ds(j * GCH, GCH)].unsqueeze(2).to_broadcast([P, GCH, S])
                V_.tensor_tensor(buf[2][:].rearrange("p t (k n) -> p (t k) n", n=S), tps[:], gsl, ALU.mult).then_inc(t_free, 1)

            def decayed(j):
                for i in range(2):
                    dve.wait_ge(rs_full, j * 2 + (i + 1))
                    V_.tensor_tensor(ptr[:, i, :], rs_ps[i][:, 0:RET_COLS], decay[:, ds(j * 2 + i, 1), :].rearrange("p a n -> p (a n)"),
                                     ALU.mult).then_inc(ptr_ready, 1)

            def stage3(j, first):
                V, G = Block(B3, 2, j), Block(B3 + 1, 2, j)
                if first:
                    split(V, 0, 4)
                    gated_attention(3)
                    split(V, 4, 8)
                    dve.wait_ge(decay_full, 16)
                    split(G, 0, 1)
                else:
                    tail3(j - 1, V)
                    split(G, 0, 1)
                    lo_from_gained(j, buf[2], tb_hi, tb_lo, j - 1, retT_ready)
                split(G, 1, 6)
                decayed(j)
                split(G, 6, 8)

            stage3(0, True)
            with dve.Fori(1, 4) as j:
                mine.enter_loop(j, 1, OWN_STAGE3)
                stage3(j, False)
            mine.leave_loop(3, OWN_STAGE3)

            def merge(j):
                B = Block(B4 + 1, 2, j)
                dve.wait_ge(unit_done, B.unit(UNITS - 1))
                mine.wait(dve)
                dve.wait_ge(t_full, j + T_STAGE4)
                V_.tensor_tensor(buf[3][:], buf[2][:], acc[0][:], ALU.mult).then_inc(evacuated[0], 1)
                dve.wait_ge(evacuated[0], B.turn + 1)
                V_.tensor_tensor(buf[3][:], buf[3][:], mix[:, :, ds(j * COLS, COLS)], ALU.add).then_inc(m_ready, 1)

            def stage4(j, first):
                G, R = Block(B4, 2, j), Block(B4 + 1, 2, j)
                if first:
                    tail3(3, G)
                    split(R, 0, 1)
                    lo_from_gained(4, buf[2], tb_hi, tb_lo, 3, retT_ready)
                else:
                    split(G, 0, 4)
                    merge(j - 1)
                    split_and_turn(G, 4, 8, j + (T_STAGE4 - 1), buf[3][:], m_ready, j)
                    lo_from_turned(j + 4, tc_hi, tc_lo, j - 1)
                    split(R, 0, 1)
                split(R, 1, 5)
                gate(G)
                split(R, 5, 8)

            stage4(0, True)
            with dve.Fori(1, 4) as j:
                mine.enter_loop(j, 1, OWN_STAGE4)
                stage4(j, False)
            mine.leave_loop(3, OWN_STAGE4)

            def add_residual(B, j):
                dve.wait_ge(unit_done, B.unit(UNITS - 1))
                sl = mix[:, :, j * COLS:(j + 1) * COLS]
                V_.tensor_tensor(sl, sl, acc[B.parity][:], ALU.add).then_inc(evacuated[B.parity], 1)

            def inverse_rms(done):
                mine.step(V_.tensor_reduce(sum2[:], ssq2[:], AX.X, ALU.add))
                mine.wait(dve)
                V_.tensor_scalar(msq[:, 0:2], sum2[:], 1.0 / D, EPS, ALU.mult, ALU.add).then_inc(done, 1)

            for j in range(GROUPS + 1):
                B = Block(B5 + j)
                split(B, 0, 4)
                if j == 0:
                    merge(3)
                else:
                    dve.wait_ge(xres_full[j - 1], 16)
                    add_residual(Block(B5 + j - 1), j - 1)
                if j == 0:
                    split_and_turn(B, 4, 8, T_STAGE4 + 3, buf[3][:], m_ready, 4)
                    lo_from_turned(8, tc_hi, tc_lo, 3)
                else:
                    prev = Block(B5 + j - 1)
                    split_and_turn(B, 4, 8, T_STAGE5 + j - 1, mix[:, :, (j - 1) * COLS:j * COLS],
                                   evacuated[prev.parity], prev.turn + 1)
                    gain(T_STAGE5 + j - 1, buf[2], gffn, j - 1)
                    lo_from_gained(8 + j, buf[2], ta_hi, ta_lo, j - 1, h2T_ready)
                if j == GROUPS:
                    dve.wait_ge(x1_sq, 4)
                    inverse_rms(ms2_ready)

            def square(B):
                dve.wait_ge(evacuated[B.parity], B.turn + 1)
                V_.tensor_tensor(buf[0][:], buf[0][:], buf[0][:], ALU.mult).then_inc(u_ready, 1)

            def add_down(q, i, B):
                if later(q):
                    dve.wait_ge(down_sq, q * 4 + (i - 3))
                add_residual(B, i)

            def stage6(q, first):
                B = [Block(B6 + i, 8, q) for i in range(8)]
                if not first:
                    split(B[0], 0, 4)
                    add_residual(Block(B6 - 1, 8, q), 3)
                    split(B[0], 4, 8)
                for i in range(1, 5):
                    split(B[i], 0, 4)
                    square(B[i - 1])
                    split_and_turn(B[i], 4, 8, q * 4 + (T_STAGE6 + i - 1), buf[0][:], u_ready, q * 4 + i)
                    lo_from_turned(q * 4 + (12 + i), tb_hi, tb_lo, i - 1)
                for i in range(5, 8):
                    split(B[i], 0, 4)
                    if not first:
                        dve.wait_ge(down_sq, q * 4 + (i - 8))
                    add_residual(B[i - 1], i - 5)
                    split(B[i], 4, 8)

            stage6(0, True)
            with dve.Fori(1, 4) as q:
                stage6(q, False)
            dve.wait_ge(fin_full, 16)

            def final_gain(j0, j1):
                cols = slice(j0 * COLS, j1 * COLS)
                V_.tensor_tensor(final[:, :, cols], mix[:, :, cols],
                                 gfin[:, cols].unsqueeze(1).to_broadcast([P, TILES, (j1 - j0) * COLS]),
                                 ALU.mult).then_inc(final_g, 1)

            for j in range(3):
                B = Block(B6 + 28 + j)
                dve.wait_ge(evacuated[B.parity], B.turn + 1)
            final_gain(0, 3)
            dve.wait_ge(down_sq, 12)
            add_residual(Block(68), 3)
            dve.wait_ge(evacuated[0], Block(68).turn + 1)
            final_gain(3, 4)
            dve.wait_ge(down_sq, 16)
            inverse_rms(ms3_ready)
            dve.wait_ge(rstd3_ready, 1)
            dve.wait_ge(final_g, 2)
            for h in range(2):
                cols = slice(h * 1024, (h + 1) * 1024)
                V_.tensor_scalar(final[:, 1, cols], final[:, 1, cols], rstd3[:, 1:2], None, ALU.mult).then_inc(final_dve, 1)

        @block.gpsimd
        def _(pool):
            nc.gpsimd.memset(mhalf[:], -0.5).then_inc(mhalf_set, 1)
            pool.wait_ge(mhalf_set, 1)
            pool.wait_ge(ms_ready, 1)
            nc.gpsimd.tensor_tensor(rstd[:], msq[:, 0:2], mhalf[:, 0:2], ALU.pow).then_inc(pow_ready, 1)
            pool.wait_ge(vshift, 1)
            for g in range(KV_HEADS):
                if g:
                    pool.wait_ge(av_full, g * NCHUNK)
                nc.gpsimd.tensor_copy(vst[:], vwin[:, :, g, :]).then_inc(vst_ready, 1)
            for j in range(4):
                pool.wait_ge(rms_ready, j + 1)
                nc.gpsimd.tensor_tensor(powr[:].rearrange("p i t -> p (i t)"), msq[:], mhalf[:], ALU.pow).then_inc(rpow_ready, 1)
            pool.wait_ge(ms2_ready, 1)
            nc.gpsimd.tensor_tensor(rstd2[:], msq[:, 0:2], mhalf[:, 0:2], ALU.pow).then_inc(rstd2_ready, 1)
            pool.wait_ge(ms3_ready, 1)
            nc.gpsimd.tensor_tensor(rstd3[:], msq[:, 0:2], mhalf[:, 0:2], ALU.pow).then_inc(rstd3_ready, 1)


def constants():
    half = RET_QK // 2
    inv = (np.float32(10000.0) ** (-np.arange(half, dtype=np.float32) / np.float32(half))).astype(np.float32)
    ang = np.arange(S, dtype=np.float32)[:, None] * inv[None, :]
    cs = np.stack([np.cos(ang), np.sin(ang)]).astype(np.float32)
    rope = np.ascontiguousarray(cs.reshape(2, TILES, P, half).transpose(2, 0, 1, 3))
    n = np.arange(S)
    lg = np.log1p(-np.exp2(-5.0 - np.arange(RET_HEADS)))
    full = np.exp(lg[:, None, None] * np.abs(n[:, None] - n[None, :])) * RET_QK ** -0.5
    full = full * (n[:, None] // CHUNK <= n[None, :] // CHUNK)
    decay = np.concatenate([full[:, :P, :], full[:, P:, P:]], axis=2).transpose(1, 0, 2)
    return np.eye(P, dtype=np.float32), rope, np.ascontiguousarray(decay.astype(np.float32))


def kernel(x, norm_mix_g, w_in, ret_norm_g, attn_sinks, w_ret_branch, w_attn_branch, w_gate, w_out,
           norm_ffn_g, w_up, w_down, norm_final_g):
    import concourse.bacc as _bacc
    from concourse.bass_utils import run_bass_kernel_spmd as _run

    nc = _bacc.Bacc("TRN2", target_bir_lowering=False, num_devices=1)
    ident, rope, decay = constants()

    def columns(g):
        return np.asarray(g).reshape(KCH, P).T

    sinks = np.repeat(np.asarray(attn_sinks).reshape(16, 2).T, P // 2, axis=0)
    small = np.concatenate([ident, rope.reshape(P, -1), columns(norm_mix_g), columns(ret_norm_g),
                            columns(norm_ffn_g), sinks], axis=1)
    given = {
        "x": np.asarray(x)[0], "x_t": np.asarray(x)[0].reshape(S, KCH, P).transpose(2, 1, 0), "w_in": np.asarray(w_in)[0],
        "w_ret": np.asarray(w_ret_branch)[0], "w_att": np.asarray(w_attn_branch)[0],
        "w_gate": np.asarray(w_gate)[0], "w_out": np.asarray(w_out)[0],
        "w_up": np.asarray(w_up)[0], "w_down": np.asarray(w_down)[0],
        "g_fin": np.asarray(norm_final_g), "small_c": small, "decay_c": decay,
    }
    arrays, args = {}, {}
    for name, a in given.items():
        arrays["in_" + name] = np.ascontiguousarray(a)
        args[name] = nc.dram_tensor("in_" + name, a.shape, mybir.dt.float32, kind="ExternalInput").ap()
    out = nc.dram_tensor("out_0", (S, D), mybir.dt.float32, kind="ExternalOutput").ap()
    build(nc, out=out, **args)
    r = _run(nc, [arrays], core_ids=[0])
    return r.results[0]["out_0"].reshape(1, S, D)
```

```python
import concourse.bass as bass
from concourse import mybir
from contextlib import ExitStack
import numpy as np

P = 128
D = 2048
S = 256
TILES = S // P
COLS = 512
KCH = D // P
UNITS = 8
UCH = KCH // UNITS
SQ = 32
LOADS = 4
GROUPS = D // COLS
GCH = COLS // P
EPS = 1e-6
CHUNK = 64
NCHUNK = S // CHUNK
RET_HEADS = 8
RET_QK = D // 16
RET_V = D // 8
ATT_D = 64
KV_HEADS = 4
RET_COLS = S + (S - P)
ATT_SCALE = ATT_D ** -0.5
OFF_RQK = 0
OFF_RV = 2 * RET_HEADS * RET_QK
OFF_RG = OFF_RV + D
OFF_AQ = OFF_RG + D
OFF_AKV = OFF_AQ + D
SMALL = P + 2 * TILES * (RET_QK // 2) + 4 * KCH
KEYS = [(0, CHUNK, 0), (0, 2 * CHUNK, 0), (CHUNK, 2 * CHUNK, 1), (2 * CHUNK, 2 * CHUNK, 2)]


class Block:

    def __init__(self, first, step=0, j=0):
        self.number = j * step + first
        self.parity = first % 2
        self.turn = j * (step // 2) + first // 2
        self.reused = first >= 2
        self.very_first = first == 0

    def unit(self, u):
        return self.number * UNITS + (u + 1)


def later(n):
    return not (type(n) is int and n == 0)


class Steps:

    def __init__(self, sem):
        self.sem, self.base, self.here, self.total = sem, 0, 0, 0

    def step(self, instruction):
        instruction.then_inc(self.sem, 1)
        self.here += 1
        self.total += 1

    def wait(self, engine):
        engine.wait_ge(self.sem, self.base + self.here)

    def enter_loop(self, j, first, per):
        self.before, self.base, self.here = self.total, j * per + (self.total - first * per), 0

    def leave_loop(self, turns, per):
        assert self.here == per, (self.here, per)
        self.total = self.before + turns * per
        self.base, self.here = self.total, 0


LAST = 68
ACT_COLS, DVE_COLS = 768, 640
WARM_UP = 16
OWN_STAGE1, OWN_STAGE2, OWN_STAGE3, OWN_STAGE4 = 18, 1, 1, 1


def build(nc, x, x_t, w_in, w_ret, w_att, w_gate, w_out, w_up, w_down, g_fin,
          small_c, decay_c, out):
    f32, f32r = mybir.dt.float32, mybir.dt.float32r
    ALU, ACT, AX = mybir.AluOpType, mybir.ActivationFunctionType, mybir.AxisListType
    ds = bass.ds

    ctx = ExitStack()
    with ctx:
        here = [(nc.sbuf_base + 63) // 64 * 64]

        def place(name, shape, dt, at=None):
            size = int(np.prod(shape[1:])) * 4
            if at is None:
                at = here[0]
                here[0] += (size + 31) // 32 * 32
            return nc.alloc_sbuf_tensor_at(name, shape, dt, offset=at)

        def sem(name):
            return ctx.enter_context(nc.semaphore(name))

        K = 1024
        at_a = here[0]
        ta_hi = place("ta_hi", [P, KCH, S], f32r)
        ta_lo = place("ta_lo", [P, KCH, S], f32r)
        at_b = here[0]
        tb_hi = place("tb_hi", [P, KCH, S], f32r)
        tb_lo = place("tb_lo", [P, KCH, S], f32r)
        at_c = here[0]
        tc_hi = place("tc_hi", [P, KCH, S], f32r)
        tc_lo = place("tc_lo", [P, KCH, S], f32r)
        at_m = here[0]
        mix = place("mix", [P, TILES, D], f32)
        raw = place("raw", [P, KCH, COLS], f32)
        whi = place("whi", [P, KCH // 2, COLS], f32r)
        wlo = place("wlo", [P, KCH // 2, COLS], f32r)
        buf = [place(f"buf{i}", [P, TILES, COLS], f32) for i in range(4)]
        gfin = place("gfin", [P, D], f32)
        kst = place("kst", [P, 2, S], f32)
        vst = place("vst", [P, 3, P], f32)
        half_qk = RET_QK // 2
        small = place("small", [P, SMALL], f32)
        ident = small[:, 0:P]
        rope = small[:, P:P + 2 * TILES * half_qk].rearrange("p (a t d) -> p a t d", a=2, t=TILES)
        gmix, gret, gffn, sink = [small[:, SMALL - (4 - i) * KCH:SMALL - (3 - i) * KCH] for i in range(4)]
        roper = place("roper", [P, 2, TILES, half_qk], f32)
        nsink = place("nsink", [P, 16], f32)
        ssq = place("ssq", [P, 2], f32)
        msq = place("msq", [P, 4], f32)
        rstd = place("rstd", [P, 2], f32)
        rstd_half = place("rstd_half", [P, 2], f32)
        ssq2 = place("ssq2", [P, TILES, GROUPS], f32)
        sum2 = place("sum2", [P, 2], f32)
        rstd2 = place("rstd2", [P, 2], f32)
        rstd3 = place("rstd3", [P, 2], f32)
        ssqr = place("ssqr", [P, 2, TILES], f32)
        powr = place("powr", [P, 2, TILES], f32)
        retsc = place("retsc", [P, 2, TILES], f32)
        mhalf = place("mhalf", [P, 4], f32)
        mx = place("mx", [P, 4], f32)
        negm = place("negm", [P, 4], f32)
        esd = place("esd", [P, 4], f32)
        es = place("es", [P, 4], f32)
        sums = place("sums", [P, 4], f32)
        den = place("den", [P, 4], f32)
        rden = place("rden", [P, 4], f32)
        assert here[0] <= nc.sbuf_usable_end, here[0]
        xin = place("xin", [P, TILES, D], f32, at_b)
        xt = place("xt", [P, KCH, S], f32, at_b + 16 * K)
        junk = place("junk", [P, D], f32, at_c + 24 * K)
        qkT = place("qkT", [P, 2 * RET_HEADS, S], f32, at_c)
        qbd = place("qbd", [P, 4, NCHUNK, P], f32, at_c + 16 * K)
        decay = place("decay", [P, RET_HEADS, RET_COLS], f32, at_c + 16 * K)
        ptr = place("ptr", [P, 2, RET_COLS], f32, at_c + 28 * K)
        final = place("final", [P, TILES, D], f32, at_c)
        kT = place("kT", [P, KV_HEADS, S], f32, at_m)
        vwin = place("vwin", [P, 3, KV_HEADS, P], f32, at_m + 4 * K)
        prob = place("prob", [P, 4, P], f32, at_m + 10 * K)
        probT = place("probT", [P, 4, P], f32, at_m + 12 * K)

        acc = [ctx.enter_context(nc.psum_tensor(f"acc{i}", [P, TILES, COLS], f32)) for i in range(2)]
        tps = ctx.enter_context(nc.psum_tensor("tps", [P, GCH, S], f32))
        sps = ctx.enter_context(nc.psum_tensor("sps", [P, 4, P], f32))
        pps = ctx.enter_context(nc.psum_tensor("pps", [P, 4, P], f32))
        flat = "p a b -> p (a b)"
        rs_ps = [sps[:].rearrange(flat), pps[:].rearrange(flat)]
        out_ps = tps[:].rearrange("p (i t) e -> p i t e", t=TILES)

        raw_full = [sem(f"raw_full{s}") for s in range(LOADS)]
        hi_ready, lo_ready, unit_done = sem("hi_ready"), sem("lo_ready"), sem("unit_done")
        evacuated = [sem("evacuated0"), sem("evacuated1")]
        xt_full = [sem(f"xt_full{u}") for u in range(UNITS)]
        first_full, x_full = sem("first_full"), sem("x_full")
        xt_gained, xt_hi = sem("xt_gained"), sem("xt_hi")
        warm = sem("warm")
        const_full, fin_full = sem("const_full"), sem("fin_full")
        decay_full = sem("decay_full")
        xres_full = [sem(f"xres_full{j}") for j in range(GROUPS)]
        r_full, r_placed = sem("r_full"), sem("r_placed")
        turned_1 = sem("turned_1")
        t_full, t_free = sem("t_full"), sem("t_free")
        ret_full, ret_read = sem("ret_full"), sem("ret_read")
        t_hi = sem("t_hi")
        hT_ready, retT_ready, h2T_ready = sem("hT_ready"), sem("retT_ready"), sem("h2T_ready")
        own = sem("own")
        mhalf_set, ssq_ready, ms_ready = sem("mhalf_set"), sem("ssq_ready"), sem("ms_ready")
        pow_ready, rstd_ready = sem("pow_ready"), sem("rstd_ready")
        consts_ready = sem("consts_ready")
        keys_ready, vshift, vst_ready, rope_ready = sem("keys_ready"), sem("vshift"), sem("vst_ready"), sem("rope_ready")
        s_full, negm_ready, exp_done, p_ready = sem("s_full"), sem("negm_ready"), sem("exp_done"), sem("p_ready")
        pt_full, pt_ready, av_full, att_hi, att_lo = sem("pt_full"), sem("pt_ready"), sem("av_full"), sem("att_hi"), sem("att_lo")
        kst_ready, rs_full, ptr_ready = sem("kst_ready"), sem("rs_full"), sem("ptr_ready")
        rssq_ready, rms_ready, rpow_ready = sem("rssq_ready"), sem("rms_ready"), sem("rpow_ready")
        rgate_ready, gated_ready = sem("rgate_ready"), sem("gated_ready")
        m_ready, u_ready = sem("m_ready"), sem("u_ready")
        x1_sq, ms2_ready, rstd2_ready = sem("x1_sq"), sem("ms2_ready"), sem("rstd2_ready")
        down_sq, ms3_ready, rstd3_ready = sem("down_sq"), sem("ms3_ready"), sem("rstd3_ready")
        tile_done, added, last_sq = sem("tile_done"), sem("added"), sem("last_sq")
        final_g, final_act, final_dve, stored = sem("final_g"), sem("final_act"), sem("final_dve"), sem("stored")

        T_Q = 1
        T_STAGE3 = 0
        T_STAGE4 = T_STAGE3 + 4
        T_STAGE5 = T_STAGE4 + 4
        T_STAGE6 = T_STAGE5 + 4
        B1, B2, B3, B4, B5, B6 = 1, 9, 17, 25, 33, 37

        spare = [a[:].rearrange("p (k n) s -> p k (n s)", n=COLS // S) for a in (ta_hi, ta_lo)]

        def last_slot(part, u):
            ring = (whi, wlo)[part]
            return ring[:, u * UCH:(u + 1) * UCH, :] if u < UNITS // 2 else spare[part][:, u * UCH - KCH // 2:(u + 1) * UCH - KCH // 2, :]

        turned = buf[1][:].rearrange("p t (m n) -> p (t m) n", n=S)

        def gained(u):
            return buf[2 + u % 2][:, 0, :].rearrange("p (k n) -> p k n", n=S)

        block = ctx.enter_context(nc.Block())

        @block.sync
        def _(sp):
            def load(B, src, s):
                src = src.rearrange("(k p) n -> p k n", p=P)
                sp.lower_ap_dma(src)
                if not B.very_first:
                    sp.wait_ge(lo_ready, B.number * UNITS + (2 * s + 2 - UNITS))
                sp.dma_start(raw[:, GCH * s:GCH * (s + 1), :],
                             src).then_inc(raw_full[s], 16)

            def load_block(B, w, col, row=0):
                for s in range(LOADS):
                    load(B, w[ds(row + s * 512, 512), ds(col, COLS)], s)

            def load_xt(u):
                ch = slice(u * UCH, (u + 1) * UCH)
                sp.dma_start(xt[:, ch, :], x_t[:, ch, :]).then_inc(xt_full[u], 16)

            load_xt(0)
            w = w_in[0:COLS, OFF_AKV:OFF_AKV + COLS].rearrange("(k p) n -> p k n", p=P)
            sp.dma_start(raw[:, 0:UCH, :], w[:, 0:UCH, :]).then_inc(first_full, 16)
            load_xt(1)
            sp.dma_start(raw[:, UCH:GCH, :], w[:, UCH:GCH, :]).then_inc(raw_full[0], 16)
            for s in range(1, LOADS):
                load_xt(2 * s)
                load(Block(0), w_in[s * 512:(s + 1) * 512, OFF_AKV:OFF_AKV + COLS], s)
                load_xt(2 * s + 1)
            for s in range(2):
                load(Block(1), w_in[s * 512:(s + 1) * 512, OFF_AQ:OFF_AQ + COLS], s)
            sp.dma_start(xin[:], x.rearrange("(t p) n -> p t n", p=P)).then_inc(x_full, 16)
            for s in range(2, LOADS):
                load(Block(1), w_in[s * 512:(s + 1) * 512, OFF_AQ:OFF_AQ + COLS], s)
            load_block(Block(2), w_in, OFF_RQK)

            def stage1(j):
                load_block(Block(B1, 2, j), w_in, j * COLS + OFF_AQ)
                load_block(Block(B1 + 1, 2, j), w_in, j * COLS + OFF_RQK)

            def stage2(j):
                load_block(Block(B2, 2, j), w_gate, j * COLS + D)
                load_block(Block(B2 + 1, 2, j), w_att, j * COLS)

            def stage3(j):
                load_block(Block(B3, 2, j), w_in, j * COLS + OFF_RV)
                load_block(Block(B3 + 1, 2, j), w_in, j * COLS + OFF_RG)

            def stage4(j):
                load_block(Block(B4, 2, j), w_gate, j * COLS)
                load_block(Block(B4 + 1, 2, j), w_ret, j * COLS)

            with sp.Fori(1, 4) as j:
                stage1(j)
            stage2(0)
            with sp.Fori(1, 4) as j:
                stage2(j)
            sp.wait_ge(s_full, 16)
            sp.dma_start(decay[:], decay_c).then_inc(decay_full, 16)
            stage3(0)
            with sp.Fori(1, 4) as j:
                stage3(j)
            sp.dma_start(gfin[:], g_fin.partition_broadcast(P)).then_inc(fin_full, 16)
            stage4(0)
            with sp.Fori(1, 4) as j:
                stage4(j)
            for j in range(GROUPS):
                if j == GROUPS - 1:
                    load_block(Block(B5), w_out, 0)
                sp.wait_ge(m_ready, j + 1)
                sp.dma_start(mix[:, :, j * COLS:(j + 1) * COLS],
                             x[:, j * COLS:(j + 1) * COLS].rearrange("(t p) n -> p t n", p=P)).then_inc(xres_full[j], 16)
            for j in range(1, GROUPS):
                load_block(Block(B5 + j), w_out, j * COLS)

            def stage6(q):
                for i in range(4):
                    load_block(Block(B6 + i, 8, q), w_up, q * D + i * COLS)
                for i in range(4):
                    load_block(Block(B6 + 4 + i, 8, q), w_down, i * COLS, q * D)

            stage6(0)
            with sp.Fori(1, 4) as q:
                stage6(q)
            for t in range(TILES):
                for h in range(2):
                    cols = slice(ACT_COLS + h * DVE_COLS, ACT_COLS + (h + 1) * DVE_COLS)
                    sp.wait_ge(final_dve, 2 * t + h + 1)
                    sp.dma_start(out[t * P:(t + 1) * P, cols], final[:, t, cols]).then_inc(stored, 16)
            sp.wait_ge(stored, 3 * TILES * 16)

        @block.tensor
        def _(pe):
            def gemm(B, hi, lo, u0, u1):
                for u in range(u0, u1):
                    if u == 0 and B.reused:
                        pe.wait_ge(evacuated[B.parity], B.turn)
                    pe.wait_ge(lo_ready, B.unit(u))
                    for kk in range(UCH):
                        k, slot = u * UCH + kk, (u * UCH + kk) % (KCH // 2)
                        for t in range(TILES):
                            tok = slice(t * P, (t + 1) * P)
                            for n, (a, b) in enumerate(((hi, whi), (hi, wlo), (lo, whi))):
                                last = nc.tensor.matmul(acc[B.parity][:, t, :], a[:, k, tok], b[:, slot, :],
                                                        start=(k == 0 and n == 0), stop=(k == KCH - 1 and n == 2))
                    last.then_inc(unit_done, 1)

            def scores(g, c):
                n = g * NCHUNK + c
                if c == 0:
                    pe.wait_ge(turned_1, g + (T_Q + 1))
                if later(n):
                    pe.wait_ge(exp_done, n)
                k0, kn, _ = KEYS[c]
                for pair in range(4):
                    last = nc.tensor.matmul(sps[:, pair, 0:kn], qbd[:, pair, c, :],
                                            kT[:, ds(g, 1), k0:k0 + kn].rearrange("p a n -> p (a n)"),
                                            start=True, stop=True)
                last.then_inc(s_full, 1)

            def prob_transposes(g, c):
                n = g * NCHUNK + c
                pe.wait_ge(p_ready, n + 1)
                if later(n):
                    pe.wait_ge(att_lo, n)
                for pair in range(4):
                    last = nc.tensor.transpose(pps[:, pair, :], prob[:, pair, :], ident)
                last.then_inc(pt_full, 1)

            def attend(g, c):
                if c == 0:
                    pe.wait_ge(vst_ready, g + 1)
                pe.wait_ge(pt_ready, g * NCHUNK + c + 1)
                nc.tensor.matmul(pps[:].rearrange(flat), vst[:, KEYS[c][2], :], probT[:].rearrange(flat),
                                 start=True, stop=True).then_inc(av_full, 1)

            pe.wait_ge(warm, 1)
            for _ in range(WARM_UP):
                nc.tensor.matmul(pps[:, 0, :], mix[:, 0, 0:P], mix[:, 0, 0:P], start=True, stop=True)
            for u in range(UNITS):
                pe.wait_ge(hT_ready, u + 1)
                gemm(Block(0), ta_hi, ta_lo, u, u + 1)

            def tail_a(g, B, hi, lo):
                gemm(B, hi, lo, 0, 1)
                attend(g, 0)
                gemm(B, hi, lo, 1, 4)
                prob_transposes(g, 1)
                scores(g, 2)
                gemm(B, hi, lo, 4, 5)
                attend(g, 1)
                pe.wait_ge(rope_ready, g + 1)
                for m in range(GCH):
                    for t in range(TILES):
                        last = nc.tensor.transpose(tps[:, m, t * P:(t + 1) * P], buf[1][:, t, m * P:(m + 1) * P], ident)
                last.then_inc(r_full, 1)
                gemm(B, hi, lo, 5, 7)
                prob_transposes(g, 2)
                scores(g, 3)
                gemm(B, hi, lo, 7, 8)
                attend(g, 2)

            def stage1(j, first):
                A, R = Block(B1, 2, j), Block(B1 + 1, 2, j)
                if first:
                    gemm(A, ta_hi, ta_lo, 0, 8)
                    pe.wait_ge(const_full, 16)
                else:
                    tail_a(j - 1, A, ta_hi, ta_lo)
                gemm(R, ta_hi, ta_lo, 0, 3)
                if not first:
                    prob_transposes(j - 1, 3)
                gemm(R, ta_hi, ta_lo, 3, 4)
                if not first:
                    attend(j - 1, 3)
                scores(j, 0)
                gemm(R, ta_hi, ta_lo, 4, 8)
                prob_transposes(j, 0)
                scores(j, 1)

            stage1(0, True)
            with pe.Fori(1, 4) as j:
                stage1(j, False)

            tail_a(3, Block(B2), ta_hi, ta_lo)
            gemm(Block(B2 + 1), tb_hi, tb_lo, 0, 3)
            prob_transposes(3, 3)
            gemm(Block(B2 + 1), tb_hi, tb_lo, 3, 4)
            attend(3, 3)
            gemm(Block(B2 + 1), tb_hi, tb_lo, 4, 6)
            pe.wait_ge(att_lo, 16)
            gemm(Block(B2 + 1), tb_hi, tb_lo, 6, 8)
            with pe.Fori(1, 4) as j:
                gemm(Block(B2, 2, j), ta_hi, ta_lo, 0, 8)
                gemm(Block(B2 + 1, 2, j), tb_hi, tb_lo, 0, 8)

            def stage3(j, first):
                V, G = Block(B3, 2, j), Block(B3 + 1, 2, j)
                gemm(V, ta_hi, ta_lo, 0, 8)
                gemm(G, ta_hi, ta_lo, 0, 2)
                pe.wait_ge(kst_ready, j + 1)
                if not first:
                    pe.wait_ge(ptr_ready, j * 2)
                for i in range(2):
                    q = qkT[:, ds(j * 2 + i, 1), :].rearrange("p a n -> p (a n)")
                    nc.tensor.matmul(rs_ps[i][:, 0:S], kst[:, i, 0:P], q, start=True, stop=True)
                    nc.tensor.matmul(rs_ps[i][:, S:RET_COLS], kst[:, i, P:S],
                                     qkT[:, ds(j * 2 + i, 1), P:S].rearrange("p a n -> p (a n)"),
                                     start=True, stop=True).then_inc(rs_full, 1)
                gemm(G, ta_hi, ta_lo, 2, 5)
                pe.wait_ge(evacuated[1], V.turn + 1)
                pe.wait_ge(ptr_ready, j * 2 + 2)
                if not first:
                    pe.wait_ge(ret_read, j)
                for i in range(2):
                    v = [buf[0][:, t, i * RET_V:(i + 1) * RET_V] for t in range(TILES)]
                    nc.tensor.matmul(out_ps[:, i, 0, :], ptr[:, i, 0:P], v[0], start=True, stop=True)
                    nc.tensor.matmul(out_ps[:, i, 1, :], ptr[:, i, P:S], v[0], start=True, stop=False)
                    last = nc.tensor.matmul(out_ps[:, i, 1, :], ptr[:, i, S:RET_COLS], v[1], start=False, stop=True)
                last.then_inc(ret_full, 1)
                gemm(G, ta_hi, ta_lo, 5, 8)

            stage3(0, True)
            with pe.Fori(1, 4) as j:
                stage3(j, False)

            def stage4(j, first):
                gemm(Block(B4, 2, j), ta_hi, ta_lo, 0, 8)
                if first:
                    pe.wait_ge(retT_ready, 3)
                    gemm(Block(B4 + 1), tb_hi, tb_lo, 0, 6)
                    pe.wait_ge(retT_ready, 4)
                    gemm(Block(B4 + 1), tb_hi, tb_lo, 6, 8)
                else:
                    gemm(Block(B4 + 1, 2, j), tb_hi, tb_lo, 0, 8)

            stage4(0, True)
            with pe.Fori(1, 4) as j:
                stage4(j, False)

            for j in range(GROUPS):
                if j == 0:
                    pe.wait_ge(t_free, T_STAGE4 + 3)
                gemm(Block(B5 + j), tc_hi, tc_lo, 0, 6)
                if j == 0:
                    pe.wait_ge(t_free, T_STAGE4 + 4)
                gemm(Block(B5 + j), tc_hi, tc_lo, 6, 8)

            def stage6(q, first, last=False):
                B = [Block(B6 + i, 8, q) for i in range(8)]
                if first:
                    pe.wait_ge(h2T_ready, 3)
                    gemm(B[0], ta_hi, ta_lo, 0, 6)
                    pe.wait_ge(h2T_ready, 4)
                    gemm(B[0], ta_hi, ta_lo, 6, 8)
                else:
                    gemm(B[0], ta_hi, ta_lo, 0, 8)
                for i in range(1, 5):
                    hi, lo = (ta_hi, ta_lo) if i < 4 else (tb_hi, tb_lo)
                    if i == 4:
                        pe.wait_ge(t_free, q * 4 + (T_STAGE6 + 3))
                    gemm(B[i], hi, lo, 0, 6)
                    if i == 4:
                        pe.wait_ge(t_free, q * 4 + (T_STAGE6 + 4))
                    gemm(B[i], hi, lo, 6, 8)
                for i in range(5, 8):
                    if i == 7 and last:
                        gemm_by_tile(Block(LAST))
                    else:
                        gemm(B[i], tb_hi, tb_lo, 0, 8)

            def gemm_by_tile(B):
                pe.wait_ge(evacuated[B.parity], B.turn)
                for t in range(TILES):
                    tok = slice(t * P, (t + 1) * P)
                    for u in range(UNITS):
                        if t == 0:
                            pe.wait_ge(lo_ready, B.unit(u))
                        for kk in range(UCH):
                            k = u * UCH + kk
                            whi_k, wlo_k = [last_slot(part, u)[:, kk, :] for part in range(2)]
                            for n, (a, b) in enumerate(((tb_hi, whi_k), (tb_hi, wlo_k), (tb_lo, whi_k))):
                                done = nc.tensor.matmul(acc[B.parity][:, t, :], a[:, k, tok], b,
                                                        start=(k == 0 and n == 0), stop=(k == KCH - 1 and n == 2))
                    done.then_inc(tile_done, 1)

            stage6(0, True)
            with pe.Fori(1, 3) as q:
                stage6(q, False)
            stage6(3, False, True)

        @block.scalar
        def _(act):
            def split(B, u0, u1):
                for u in range(u0, u1):
                    if B.very_first and u == 0:
                        act.wait_ge(first_full, 16)
                    elif u % 2 == 0 or (B.very_first and u == 1):
                        act.wait_ge(raw_full[u // 2], B.number * 16 + 16)
                    if not B.very_first or u >= 4:
                        act.wait_ge(unit_done, B.unit(u - 4))
                    s = u * UCH % (KCH // 2)
                    nc.scalar.activation(whi[:, s:s + UCH, :], raw[:, u * UCH:(u + 1) * UCH, :],
                                         ACT.Copy).then_inc(hi_ready, 1)

            def scaled(B, dst, func, scale):
                act.wait_ge(unit_done, B.unit(UNITS - 1))
                for t in range(TILES):
                    last = nc.scalar.activation(dst[:, t, :], acc[B.parity][:, t, :], func, scale=scale[:, t:t + 1])
                return last

            def hi_from_turned(turn, dst, g):
                act.wait_ge(t_full, turn + 1)
                nc.scalar.activation(dst[:, ds(g * GCH, GCH), :], turned, ACT.Copy).then_inc(t_hi, 1)

            def hi_from_gained(turn, src, dst, g):
                act.wait_ge(t_free, turn + 1)
                nc.scalar.activation(dst[:, ds(g * GCH, GCH), :], src[:].rearrange("p t (k n) -> p (t k) n", n=S),
                                     ACT.Copy).then_inc(t_hi, 1)

            def exps(g, c):
                n = g * NCHUNK + c
                kn = KEYS[c][1]
                act.wait_ge(negm_ready, n + 1)
                if c:
                    act.wait_ge(pt_full, n)
                for pair in range(4):
                    nc.scalar.activation(prob[:, pair, 0:kn], sps[:, pair, 0:kn], ACT.Exp, scale=ATT_SCALE,
                                         bias=negm[:, pair:pair + 1], accum_out=sums[:, pair:pair + 1])
                nc.scalar.activation(es[:], esd[:], ACT.Exp).then_inc(exp_done, 1)

            def probs_out(g, c):
                n = g * NCHUNK + c
                act.wait_ge(pt_full, n + 1)
                if c:
                    act.wait_ge(av_full, n)
                nc.scalar.activation(probT[:], pps[:], ACT.Copy).then_inc(pt_ready, 1)

            def attended_hi(g, c):
                act.wait_ge(av_full, g * NCHUNK + c + 1)
                v = pps[:].rearrange("p a (h q) -> p a h q", h=2)
                for h in range(2):
                    part = slice(h * 64, h * 64 + 64)
                    last = nc.scalar.activation(tb_hi[part, ds(g * GCH, GCH), c * CHUNK:(c + 1) * CHUNK],
                                                v[part, :, h, :], ACT.Copy)
                last.then_inc(att_hi, 1)

            act.dma_start(small[:], small_c).then_inc(const_full, 16)

            B = Block(0)
            for u in range(UNITS):
                if u % 2:
                    split(B, u, u + 1)
                act.wait_ge(xt_gained, u + 1)
                nc.scalar.activation(ta_hi[:, u * UCH:(u + 1) * UCH, :], gained(u), ACT.Copy).then_inc(xt_hi, 1)
                if u % 2 == 0:
                    split(B, u, u + 1)

            def tail_a(g, B):
                split(B, 0, 1)
                exps(g, 0)
                split(B, 1, 4)
                probs_out(g, 0)
                split(B, 4, 5)
                exps(g, 1)
                attended_hi(g, 0)
                split(B, 5, 8)
                probs_out(g, 1)

            def tail_r(g, B):
                split(B, 0, 1)
                exps(g, 2)
                attended_hi(g, 1)
                split(B, 1, 3)
                probs_out(g, 2)
                split(B, 3, 4)
                exps(g, 3)
                attended_hi(g, 2)

            def stage1(j, first):
                A, R = Block(B1, 2, j), Block(B1 + 1, 2, j)
                if first:
                    split(A, 0, 4)
                    act.wait_ge(x_full, 16)
                    for t in range(TILES):
                        if t:
                            act.wait_ge(ssq_ready, t)
                        nc.scalar.activation(junk[:], xin[:, t, :], ACT.Square, accum_out=ssq[:, t:t + 1]).then_inc(ssq_ready, 1)
                        split(A, 4 + t, 5 + t)
                    act.wait_ge(rstd_ready, 1)
                    act.wait_ge(unit_done, Block(0).unit(UNITS - 1))
                    kd = buf[1][:].rearrange("p t (g e d) -> p t g e d", e=2, d=ATT_D)
                    vd = vwin[:].rearrange("p w g (e d) -> p w g e d", e=2)
                    kv = [acc[0][:, t, :].rearrange("p (s g d) -> p s g d", s=2, d=ATT_D) for t in range(TILES)]
                    twice = [(t, e) for t in range(TILES) for e in range(2)]
                    for t, e in twice:
                        last = nc.scalar.activation(kd[:, t, :, e, :], kv[t][:, 0], ACT.Copy, scale=rstd[:, t:t + 1])
                    last.then_inc(keys_ready, 1)
                    for t, e in twice:
                        last = nc.scalar.activation(vd[:, 2 * t, :, e, :], kv[t][:, 1], ACT.Copy, scale=rstd[:, t:t + 1])
                    last.then_inc(evacuated[0], 1)
                    split(A, 6, 8)
                    split(R, 0, 4)
                else:
                    tail_a(j - 1, A)
                    tail_r(j - 1, R)
                    act.wait_ge(turned_1, j + T_Q)
                scaled(A, buf[0], ACT.Copy, rstd).then_inc(evacuated[1], 1)
                split(R, 4, 7)
                if not first:
                    probs_out(j - 1, 3)
                split(R, 7, 8)
                if not first:
                    attended_hi(j - 1, 3)

            stage1(0, True)
            with act.Fori(1, 4) as j:
                stage1(j, False)

            tail_a(3, Block(B2))
            tail_r(3, Block(B2 + 1))
            act.wait_ge(r_placed, 4)
            scaled(Block(B2), buf[2], ACT.Tanh, rstd_half).then_inc(evacuated[1], 1)
            split(Block(B2 + 1), 4, 7)
            probs_out(3, 3)
            split(Block(B2 + 1), 7, 8)
            attended_hi(3, 3)
            with act.Fori(1, 4) as j:
                G, A = Block(B2, 2, j), Block(B2 + 1, 2, j)
                split(G, 0, 8)
                split(A, 0, 4)
                act.wait_ge(evacuated[0], A.turn)
                scaled(G, buf[2], ACT.Tanh, rstd_half).then_inc(evacuated[1], 1)
                split(A, 4, 8)

            def retention_squares(j, B):
                act.wait_ge(ret_full, j + 1)
                for i in range(2):
                    for t in range(TILES):
                        last = nc.scalar.activation(junk3[:, i, t, :], out_ps[:, i, t, :], ACT.Square,
                                                    accum_out=ssqr[:, i, t:t + 1])
                last.then_inc(rssq_ready, 1)

            junk3 = buf[3][:].rearrange("p t (i e) -> p i t e", i=2)

            def tail3(j, B):
                split(B, 0, 1)
                retention_squares(j, B)
                split(B, 1, 4)
                scaled(Block(B3 + 1, 2, j), buf[2], ACT.Tanh, rstd_half).then_inc(rgate_ready, 1)
                split(B, 4, 8)

            def stage3(j, first):
                V, G = Block(B3, 2, j), Block(B3 + 1, 2, j)
                if first:
                    split(V, 0, 8)
                    act.wait_ge(r_placed, 4)
                else:
                    tail3(j - 1, V)
                    act.wait_ge(rs_full, j * 2)
                nc.scalar.activation(kst[:], qkT[:, ds(j * 2 + RET_HEADS, 2), :], ACT.Copy).then_inc(kst_ready, 1)
                split(G, 0, 2)
                if not first:
                    hi_from_gained(j + (T_STAGE3 - 1), buf[2], tb_hi, j - 1)
                split(G, 2, 4)
                if not first:
                    act.wait_ge(ret_full, j)
                scaled(V, buf[0], ACT.Copy, rstd).then_inc(evacuated[1], 1)
                split(G, 4, 8)

            stage3(0, True)
            with act.Fori(1, 4) as j:
                stage3(j, False)

            def stage4(j, first):
                G, R = Block(B4, 2, j), Block(B4 + 1, 2, j)
                if first:
                    tail3(3, G)
                else:
                    split(G, 0, 8)
                    hi_from_turned(j + (T_STAGE4 - 1), tc_hi, j - 1)
                split(R, 0, 2)
                if first:
                    hi_from_gained(T_STAGE3 + 3, buf[2], tb_hi, 3)
                split(R, 2, 4)
                if first:
                    act.wait_ge(retT_ready, 4)
                else:
                    act.wait_ge(evacuated[0], R.turn)
                scaled(G, buf[2], ACT.Tanh, rstd_half).then_inc(evacuated[1], 1)
                split(R, 4, 8)

            stage4(0, True)
            with act.Fori(1, 4) as j:
                stage4(j, False)

            def residual_squares(B, j, done):
                act.wait_ge(evacuated[B.parity], B.turn + 1)
                for t in range(TILES):
                    last = nc.scalar.activation(buf[3][:, t, :], mix[:, t, j * COLS:(j + 1) * COLS], ACT.Square,
                                                accum_out=ssq2[:, t, j:j + 1])
                last.then_inc(done, 1)

            for j in range(GROUPS + 1):
                B = Block(B5 + j)
                split(B, 0, 5)
                if j:
                    if j == 1:
                        act.wait_ge(t_full, T_STAGE4 + 4)
                    residual_squares(Block(B5 + j - 1), j - 1, x1_sq)
                split(B, 5, 7)
                if j == 0:
                    hi_from_turned(T_STAGE4 + 3, tc_hi, 3)
                else:
                    hi_from_gained(T_STAGE5 + j - 1, buf[2], ta_hi, j - 1)
                split(B, 7, 8)

            def stage6(q, first, last=False):
                B = [Block(B6 + i, 8, q) for i in range(8)]
                if not first:
                    split(B[0], 0, 5)
                    residual_squares(Block(B6 - 1, 8, q), 3, down_sq)
                    split(B[0], 5, 8)
                for i in range(1, 5):
                    split(B[i], 0, 4)
                    if first and i == 1:
                        act.wait_ge(rstd2_ready, 1)
                    else:
                        act.wait_ge(t_full, q * 4 + (T_STAGE6 + i - 1))
                    scaled_relu(B[i - 1])
                    split(B[i], 4, 8)
                    hi_from_turned(q * 4 + (T_STAGE6 + i - 1), tb_hi, i - 1)
                for i in range(5, 8):
                    if i == 7 and last:
                        split_last(B[i])
                    else:
                        split(B[i], 0, 5)
                    residual_squares(B[i - 1], i - 5, down_sq)
                    if i < 7 or not last:
                        split(B[i], 5, 8)

            def split_last(B):
                for u in range(UNITS):
                    if u % 2 == 0:
                        act.wait_ge(raw_full[u // 2], B.number * 16 + 16)
                    if u < UNITS // 2:
                        act.wait_ge(unit_done, B.unit(u - 4))
                    nc.scalar.activation(last_slot(0, u), raw[:, u * UCH:(u + 1) * UCH, :], ACT.Copy).then_inc(hi_ready, 1)

            def scaled_relu(B):
                scaled(B, buf[0], ACT.Relu, rstd2).then_inc(evacuated[B.parity], 1)

            stage6(0, True)
            with act.Fori(1, 3) as q:
                stage6(q, False)
            stage6(3, False, True)
            j = GROUPS - 1
            for t in range(TILES):
                act.wait_ge(added, t + 1)
                nc.scalar.activation(buf[3][:, t, :], mix[:, t, j * COLS:(j + 1) * COLS], ACT.Square,
                                     accum_out=ssq2[:, t, j:j + 1]).then_inc(last_sq, 1)
                act.wait_ge(rstd3_ready, t + 1)
                act.wait_ge(final_g, 1)
                nc.scalar.activation(final[:, t, 0:ACT_COLS], final[:, t, 0:ACT_COLS], ACT.Copy,
                                     scale=rstd3[:, t:t + 1]).then_inc(final_act, 1)
                act.wait_ge(final_act, t + 1)
                act.dma_start(out[t * P:(t + 1) * P, 0:ACT_COLS], final[:, t, 0:ACT_COLS]).then_inc(stored, 16)

        @block.vector
        def _(dve):
            V_ = nc.vector
            mine = Steps(own)

            def split(B, u0, u1):
                for u in range(u0, u1):
                    dve.wait_ge(hi_ready, B.unit(u))
                    s = u * UCH % (KCH // 2)
                    V_.tensor_tensor(wlo[:, s:s + UCH, :], raw[:, u * UCH:(u + 1) * UCH, :],
                                     whi[:, s:s + UCH, :].bitcast(f32), ALU.subtract).then_inc(lo_ready, 1)

            pieces = [(i, o) for i in range(0, P, SQ) for o in range(0, P, SQ)]

            def turn(src, dst, n0, n1, done=None):
                for i, o in pieces[n0:n1]:
                    last = V_.transpose(dst(i, o), src[i:i + SQ, :, :, o:o + SQ])
                if done:
                    last.then_inc(done, 1)

            def by_chunk(src):
                return src.rearrange("p t (m f) -> p m t f", f=P)

            def to_tokens(dst):
                dst = dst.rearrange("p m (t n) -> p m t n", n=P)
                return lambda i, o: dst[o:o + SQ, :, :, i:i + SQ]

            def to_qbd(i, o):
                at = o // CHUNK * CHUNK + i % CHUNK
                return qbd[o:o + SQ].rearrange("p m (t c) n -> p m t c n", t=TILES)[:, :, :, i // CHUNK, at:at + SQ]

            def split_and_turn(B, u0, u1, before, src, ready, n):
                dve.wait_ge(ready, n)
                dve.wait_ge(t_free, before)
                for u in range(u0, u1):
                    at = [16 * (u - u0 + i) // (u1 - u0) for i in range(2)]
                    turn(by_chunk(src), to_tokens(turned), at[0], at[1], t_full if u == u1 - 1 else None)
                    split(B, u, u + 1)

            def gain(turn, dst, gains, g):
                dve.wait_ge(t_full, turn + 1)
                gsl = gains[:, ds(g * GCH, GCH)].unsqueeze(2).to_broadcast([P, GCH, S])
                V_.tensor_tensor(dst[:].rearrange("p t (k n) -> p (t k) n", n=S), turned, gsl, ALU.mult).then_inc(t_free, 1)

            def lo_from_gained(n, src, hi, lo, g, done):
                dve.wait_ge(t_hi, n)
                V_.tensor_tensor(lo[:, ds(g * GCH, GCH), :], src[:].rearrange("p t (k n) -> p (t k) n", n=S),
                                 hi[:, ds(g * GCH, GCH), :].bitcast(f32), ALU.subtract).then_inc(done, 1)

            def lo_from_turned(n, hi, lo, g):
                dve.wait_ge(t_hi, n)
                V_.tensor_tensor(lo[:, ds(g * GCH, GCH), :], turned, hi[:, ds(g * GCH, GCH), :].bitcast(f32),
                                 ALU.subtract).then_inc(t_free, 1)

            V_.memset(mix[:, 0, 0:P], 0.0).then_inc(warm, 1)
            V_.memset(qbd[:], 0.0).then_inc(consts_ready, 1)
            dve.wait_ge(const_full, 16)
            B = Block(0)

            def gain_xt(u):
                ch = slice(u * UCH, (u + 1) * UCH)
                dve.wait_ge(xt_full[u], 16)
                if u >= 2:
                    dve.wait_ge(hT_ready, u - 1)
                V_.tensor_tensor(gained(u), xt[:, ch, :], gmix[:, ch].unsqueeze(2).to_broadcast([P, UCH, S]),
                                 ALU.mult).then_inc(xt_gained, 1)

            gain_xt(0)
            for u in range(UNITS):
                ch = slice(u * UCH, (u + 1) * UCH)
                if u % 2:
                    split(B, u, u + 1)
                if 0 < u < UNITS - 1:
                    gain_xt(u + 1)
                dve.wait_ge(xt_hi, u + 1)
                V_.tensor_tensor(ta_lo[:, ch, :], gained(u), ta_hi[:, ch, :].bitcast(f32), ALU.subtract).then_inc(hT_ready, 1)
                if u % 2 == 0:
                    split(B, u, u + 1)
                if u == 0:
                    gain_xt(1)
            mine.step(V_.tensor_scalar(nsink[:], sink, -1.0, None, ALU.mult))

            def maxima(g, c):
                n = g * NCHUNK + c
                dve.wait_ge(s_full, n + 1)
                if later(n):
                    dve.wait_ge(exp_done, n)
                mine.step(V_.tensor_reduce(mx[:], sps[:, :, 0:KEYS[c][1]], AX.X, ALU.max))
                mine.wait(dve)
                mine.step(V_.scalar_tensor_tensor(negm[:], mx[:], -ATT_SCALE, nsink[:, ds(g * 4, 4)], ALU.mult, ALU.min))
                mine.wait(dve)
                V_.tensor_tensor(esd[:], negm[:], nsink[:, ds(g * 4, 4)], ALU.subtract).then_inc(negm_ready, 1)

            def normalise(g, c):
                n = g * NCHUNK + c
                kn = KEYS[c][1]
                dve.wait_ge(exp_done, n + 1)
                mine.step(V_.tensor_tensor(den[:], sums[:], es[:], ALU.add))
                mine.wait(dve)
                mine.step(V_.reciprocal(rden[:], den[:]))
                if c == 0:
                    mine.step(V_.memset(prob[:, :, kn:P], 0.0))
                mine.wait(dve)
                V_.tensor_tensor(prob[:, :, 0:kn], prob[:, :, 0:kn], rden[:].unsqueeze(2).to_broadcast([P, 4, kn]),
                                 ALU.mult).then_inc(p_ready, 1)

            def attended_lo(g, c):
                dve.wait_ge(att_hi, g * NCHUNK + c + 1)
                v = pps[:].rearrange("p a (h q) -> p a h q", h=2)
                for h in range(2):
                    part = slice(h * 64, h * 64 + 64)
                    at = (part, ds(g * GCH, GCH), slice(c * CHUNK, (c + 1) * CHUNK))
                    last = V_.tensor_tensor(tb_lo[at], v[part, :, h, :], tb_hi[at].bitcast(f32), ALU.subtract)
                last.then_inc(att_lo, 1)

            def rotate(g, B):
                dve.wait_ge(unit_done, B.unit(UNITS - 1))
                half = RET_QK // 2
                v = acc[B.parity][:].rearrange("p t (h x d) -> p t h x d", x=2, d=half)
                cos = roper[:, 0].unsqueeze(2).to_broadcast([P, TILES, 4, half])
                sin = roper[:, 1].unsqueeze(2).to_broadcast([P, TILES, 4, half])
                o = buf[1][:].rearrange("p t (h x d) -> p t h x d", x=2, d=half)
                tmp = [b[:].rearrange("p t (h d) -> p t h d", d=half)[:, :, 4 * i:4 * i + 4, :]
                       for b in (buf[2], buf[3]) for i in range(2)]
                V_.tensor_tensor(tmp[0], v[:, :, :, 0, :], cos, ALU.mult)
                V_.tensor_tensor(tmp[1], v[:, :, :, 1, :], sin, ALU.mult)
                mine.step(V_.tensor_tensor(tmp[2], v[:, :, :, 1, :], cos, ALU.mult))
                V_.tensor_tensor(tmp[3], v[:, :, :, 0, :], sin, ALU.mult).then_inc(evacuated[B.parity], 1)
                dve.wait_ge(turned_1, g + T_Q)
                dve.wait_ge(evacuated[B.parity], B.turn + 1)
                V_.tensor_tensor(o[:, :, :, 0, :], tmp[0], tmp[1], ALU.subtract)
                V_.tensor_tensor(o[:, :, :, 1, :], tmp[2], tmp[3], ALU.add).then_inc(rope_ready, 1)

            def tail_a(g, B, R):
                split(B, 0, 2)
                normalise(g, 0)
                split(B, 2, 4)
                maxima(g, 1)
                rotate(g, R)
                split(B, 4, 6)
                normalise(g, 1)
                attended_lo(g, 0)
                split(B, 6, 8)
                maxima(g, 2)

            def tail_r(g, B):
                split(B, 0, 1)
                dve.wait_ge(r_full, g + 1)
                V_.tensor_copy(qkT[:, ds(g * 4, 4), :], tps[:]).then_inc(r_placed, 1)
                normalise(g, 2)
                attended_lo(g, 1)
                split(B, 1, 3)
                maxima(g, 3)
                split(B, 3, 4)
                normalise(g, 3)
                attended_lo(g, 2)

            def stage1(j, first):
                A, R = Block(B1, 2, j), Block(B1 + 1, 2, j)
                if first:
                    split(A, 0, 5)
                    dve.wait_ge(ssq_ready, 2)
                    V_.tensor_scalar(msq[:, 0:2], ssq[:], 1.0 / D, EPS, ALU.mult, ALU.add).then_inc(ms_ready, 1)
                    dve.wait_ge(pow_ready, 1)
                    V_.tensor_scalar(rstd_half[:], rstd[:], 0.5, None, ALU.mult).then_inc(rstd_ready, 1)
                    split(A, 5, 6)
                    mine.step(V_.tensor_tensor(roper[:], rope,
                                               rstd[:].unsqueeze(1).unsqueeze(3).to_broadcast([P, 2, TILES, RET_QK // 2]), ALU.mult))
                    dve.wait_ge(keys_ready, 1)
                    turn(by_chunk(buf[1][:]), to_tokens(kT[:]), 0, 4)
                    dve.wait_ge(evacuated[0], 1)
                    V_.tensor_copy(vwin[0:64, 1], vwin[64:128, 0])
                    V_.tensor_copy(vwin[64:128, 1], vwin[0:64, 2]).then_inc(vshift, 1)
                    split(A, 6, 7)
                    turn(by_chunk(buf[1][:]), to_tokens(kT[:]), 4, 8)
                    split(A, 7, 8)
                    turn(by_chunk(buf[1][:]), to_tokens(kT[:]), 8, 12)
                    split(R, 0, 1)
                    turn(by_chunk(buf[1][:]), to_tokens(kT[:]), 12, 16, turned_1)
                    split(R, 1, 4)
                else:
                    tail_a(j - 1, A, Block(B1 + 1, 2, j - 1))
                    tail_r(j - 1, R)
                dve.wait_ge(evacuated[1], A.turn + 1)
                if first:
                    dve.wait_ge(consts_ready, 1)
                for u in range(4, 7):
                    turn(by_chunk(buf[0][:]), to_qbd, 5 * (u - 4), 16 if u == 6 else 5 * (u - 3), turned_1 if u == 6 else None)
                    split(R, u, u + 1)
                split(R, 7, 8)
                if not first:
                    attended_lo(j - 1, 3)
                maxima(j, 0)

            stage1(0, True)
            with dve.Fori(1, 4) as j:
                mine.enter_loop(j, 1, OWN_STAGE1)
                stage1(j, False)
            mine.leave_loop(3, OWN_STAGE1)

            def gate(B):
                dve.wait_ge(evacuated[1], B.turn + 1)
                mine.step(V_.tensor_scalar(buf[2][:], buf[2][:], 0.5, 0.5, ALU.mult, ALU.add))

            def gated_attention(j):
                B = Block(B2 + 1, 2, j)
                dve.wait_ge(unit_done, B.unit(UNITS - 1))
                mine.wait(dve)
                V_.tensor_tensor(mix[:, :, ds(j * COLS, COLS)], buf[2][:], acc[0][:], ALU.mult).then_inc(evacuated[0], 1)

            tail_a(3, Block(B2), Block(B2 - 1))
            tail_r(3, Block(B2 + 1))
            split(Block(B2 + 1), 4, 5)
            gate(Block(B2))
            split(Block(B2 + 1), 5, 8)
            attended_lo(3, 3)
            with dve.Fori(1, 4) as j:
                mine.enter_loop(j, 1, OWN_STAGE2)
                split(Block(B2, 2, j), 0, 4)
                gated_attention(j - 1)
                split(Block(B2, 2, j), 4, 8)
                split(Block(B2 + 1, 2, j), 0, 5)
                gate(Block(B2, 2, j))
                split(Block(B2 + 1, 2, j), 5, 8)
            mine.leave_loop(3, OWN_STAGE2)

            def tail3(j, B):
                split(B, 0, 2)
                dve.wait_ge(rssq_ready, j + 1)
                V_.tensor_scalar(msq[:], ssqr[:].rearrange("p i t -> p (i t)"), 1.0 / RET_V, EPS, ALU.mult, ALU.add).then_inc(rms_ready, 1)
                split(B, 2, 3)
                dve.wait_ge(rpow_ready, j + 1)
                mine.step(V_.tensor_tensor(retsc[:], powr[:], rstd_half[:].unsqueeze(1).to_broadcast([P, 2, TILES]), ALU.mult))
                mine.wait(dve)
                V_.tensor_tensor(buf[1][:].rearrange("p t (i e) -> p i t e", i=2), out_ps,
                                 retsc[:].unsqueeze(3).to_broadcast([P, 2, TILES, RET_V]), ALU.mult).then_inc(ret_read, 1)
                split(B, 3, 4)
                dve.wait_ge(rgate_ready, j + 1)
                dve.wait_ge(ret_read, j + 1)
                V_.tensor_tensor(buf[3][:], buf[1][:], acc[0][:], ALU.mult).then_inc(evacuated[0], 1)
                dve.wait_ge(evacuated[0], Block(B3 + 1, 2, j).turn + 1)
                V_.scalar_tensor_tensor(buf[3][:].rearrange(flat), buf[2][:].rearrange(flat), 1.0,
                                        buf[3][:].rearrange(flat), ALU.add, ALU.mult).then_inc(gated_ready, 1)
                split(B, 4, 5)
                dve.wait_ge(gated_ready, j + 1)
                for u in range(5, 8):
                    turn(by_chunk(buf[3][:]), to_tokens(turned), 4 * (u - 5), 4 * (u - 4))
                    split(B, u, u + 1)

            def after3(j, B):
                turn(by_chunk(buf[3][:]), to_tokens(turned), 12, 16, t_full)
                split(B, 0, 1)
                gain(j + T_STAGE3, buf[2], gret, j)
                split(B, 1, 2)
                lo_from_gained(j + 1, buf[2], tb_hi, tb_lo, j, retT_ready)

            def decayed(j):
                for i in range(2):
                    dve.wait_ge(rs_full, j * 2 + (i + 1))
                    V_.tensor_tensor(ptr[:, i, :], rs_ps[i][:, 0:RET_COLS], decay[:, ds(j * 2 + i, 1), :].rearrange("p a n -> p (a n)"),
                                     ALU.mult).then_inc(ptr_ready, 1)

            def stage3(j, first):
                V, G = Block(B3, 2, j), Block(B3 + 1, 2, j)
                if first:
                    split(V, 0, 4)
                    gated_attention(3)
                    split(V, 4, 8)
                    dve.wait_ge(decay_full, 16)
                    split(G, 0, 2)
                else:
                    tail3(j - 1, V)
                    after3(j - 1, G)
                split(G, 2, 6)
                decayed(j)
                split(G, 6, 8)

            stage3(0, True)
            with dve.Fori(1, 4) as j:
                mine.enter_loop(j, 1, OWN_STAGE3)
                stage3(j, False)
            mine.leave_loop(3, OWN_STAGE3)

            def merge(j):
                B = Block(B4 + 1, 2, j)
                dve.wait_ge(unit_done, B.unit(UNITS - 1))
                mine.wait(dve)
                dve.wait_ge(t_full, j + T_STAGE4)
                V_.tensor_tensor(buf[3][:], buf[2][:], acc[0][:], ALU.mult).then_inc(evacuated[0], 1)
                dve.wait_ge(evacuated[0], B.turn + 1)
                V_.tensor_tensor(buf[3][:], buf[3][:], mix[:, :, ds(j * COLS, COLS)], ALU.add).then_inc(m_ready, 1)

            def stage4(j, first):
                G, R = Block(B4, 2, j), Block(B4 + 1, 2, j)
                if first:
                    tail3(3, G)
                    after3(3, R)
                else:
                    split(G, 0, 4)
                    merge(j - 1)
                    split_and_turn(G, 4, 8, j + (T_STAGE4 - 1), buf[3][:], m_ready, j)
                    lo_from_turned(j + 4, tc_hi, tc_lo, j - 1)
                    split(R, 0, 2)
                split(R, 2, 5)
                gate(G)
                split(R, 5, 8)

            stage4(0, True)
            with dve.Fori(1, 4) as j:
                mine.enter_loop(j, 1, OWN_STAGE4)
                stage4(j, False)
            mine.leave_loop(3, OWN_STAGE4)

            def add_residual(B, j):
                dve.wait_ge(unit_done, B.unit(UNITS - 1))
                sl = mix[:, :, j * COLS:(j + 1) * COLS]
                V_.tensor_tensor(sl, sl, acc[B.parity][:], ALU.add).then_inc(evacuated[B.parity], 1)

            def inverse_rms(done):
                mine.step(V_.tensor_reduce(sum2[:], ssq2[:], AX.X, ALU.add))
                mine.wait(dve)
                V_.tensor_scalar(msq[:, 0:2], sum2[:], 1.0 / D, EPS, ALU.mult, ALU.add).then_inc(done, 1)

            for j in range(GROUPS + 1):
                B = Block(B5 + j)
                split(B, 0, 4)
                if j == 0:
                    merge(3)
                else:
                    dve.wait_ge(xres_full[j - 1], 16)
                    add_residual(Block(B5 + j - 1), j - 1)
                if j == 0:
                    split_and_turn(B, 4, 6, T_STAGE4 + 3, buf[3][:], m_ready, 4)
                    split(B, 6, 7)
                    lo_from_turned(8, tc_hi, tc_lo, 3)
                else:
                    prev = Block(B5 + j - 1)
                    split_and_turn(B, 4, 6, T_STAGE5 + j - 1, mix[:, :, (j - 1) * COLS:j * COLS],
                                   evacuated[prev.parity], prev.turn + 1)
                    gain(T_STAGE5 + j - 1, buf[2], gffn, j - 1)
                    split(B, 6, 7)
                    lo_from_gained(8 + j, buf[2], ta_hi, ta_lo, j - 1, h2T_ready)
                split(B, 7, 8)
                if j == GROUPS:
                    dve.wait_ge(x1_sq, 4)
                    inverse_rms(ms2_ready)

            def square(B):
                dve.wait_ge(evacuated[B.parity], B.turn + 1)
                V_.tensor_tensor(buf[0][:], buf[0][:], buf[0][:], ALU.mult).then_inc(u_ready, 1)

            def stage6(q, first, last=False):
                B = [Block(B6 + i, 8, q) for i in range(8)]
                if not first:
                    split(B[0], 0, 4)
                    add_residual(Block(B6 - 1, 8, q), 3)
                    split(B[0], 4, 8)
                for i in range(1, 5):
                    split(B[i], 0, 4)
                    square(B[i - 1])
                    split_and_turn(B[i], 4, 8, q * 4 + (T_STAGE6 + i - 1), buf[0][:], u_ready, q * 4 + i)
                    lo_from_turned(q * 4 + (12 + i), tb_hi, tb_lo, i - 1)
                for i in range(5, 8):
                    if i == 7 and last:
                        split_last(B[i])
                    else:
                        split(B[i], 0, 4)
                    if not first:
                        dve.wait_ge(down_sq, q * 4 + (i - 8))
                    add_residual(B[i - 1], i - 5)
                    if i < 7 or not last:
                        split(B[i], 4, 8)

            def split_last(B):
                for u in range(UNITS):
                    dve.wait_ge(hi_ready, B.unit(u))
                    V_.tensor_tensor(last_slot(1, u), raw[:, u * UCH:(u + 1) * UCH, :],
                                     last_slot(0, u).bitcast(f32), ALU.subtract).then_inc(lo_ready, 1)

            stage6(0, True)
            with dve.Fori(1, 3) as q:
                stage6(q, False)
            stage6(3, False, True)
            dve.wait_ge(fin_full, 16)
            for B in (Block(LAST - 3), Block(LAST - 2), Block(LAST - 1)):
                dve.wait_ge(evacuated[B.parity], B.turn + 1)
            early = (GROUPS - 1) * COLS
            V_.tensor_tensor(final[:, :, 0:early], mix[:, :, 0:early],
                             gfin[:, 0:early].unsqueeze(1).to_broadcast([P, TILES, early]), ALU.mult).then_inc(final_g, 1)
            dve.wait_ge(down_sq, 15)
            for t in range(TILES):
                sl = mix[:, t, early:D]
                dve.wait_ge(tile_done, t + 1)
                V_.tensor_tensor(sl, sl, acc[0][:, t, :], ALU.add).then_inc(added, 1)
                dve.wait_ge(added, t + 1)
                V_.tensor_tensor(final[:, t, early:D], sl, gfin[:, early:D], ALU.mult).then_inc(final_g, 1)
                dve.wait_ge(last_sq, t + 1)
                mine.step(V_.tensor_reduce(sum2[:, t:t + 1], ssq2[:, t, :], AX.X, ALU.add))
                mine.wait(dve)
                V_.tensor_scalar(msq[:, t:t + 1], sum2[:, t:t + 1], 1.0 / D, EPS, ALU.mult, ALU.add).then_inc(ms3_ready, 1)
                dve.wait_ge(rstd3_ready, t + 1)
                dve.wait_ge(final_g, t + 2)
                for h in range(2):
                    cols = slice(ACT_COLS + h * DVE_COLS, ACT_COLS + (h + 1) * DVE_COLS)
                    V_.tensor_scalar(final[:, t, cols], final[:, t, cols], rstd3[:, t:t + 1], None, ALU.mult).then_inc(final_dve, 1)

        @block.gpsimd
        def _(pool):
            nc.gpsimd.memset(mhalf[:], -0.5).then_inc(mhalf_set, 1)
            pool.wait_ge(mhalf_set, 1)
            pool.wait_ge(ms_ready, 1)
            nc.gpsimd.tensor_tensor(rstd[:], msq[:, 0:2], mhalf[:, 0:2], ALU.pow).then_inc(pow_ready, 1)
            pool.wait_ge(vshift, 1)
            for g in range(KV_HEADS):
                if g:
                    pool.wait_ge(av_full, g * NCHUNK)
                nc.gpsimd.tensor_copy(vst[:], vwin[:, :, g, :]).then_inc(vst_ready, 1)
            for j in range(4):
                pool.wait_ge(rms_ready, j + 1)
                nc.gpsimd.tensor_tensor(powr[:].rearrange("p i t -> p (i t)"), msq[:], mhalf[:], ALU.pow).then_inc(rpow_ready, 1)
            pool.wait_ge(ms2_ready, 1)
            nc.gpsimd.tensor_tensor(rstd2[:], msq[:, 0:2], mhalf[:, 0:2], ALU.pow).then_inc(rstd2_ready, 1)
            for t in range(TILES):
                pool.wait_ge(ms3_ready, t + 1)
                nc.gpsimd.tensor_tensor(rstd3[:, t:t + 1], msq[:, t:t + 1], mhalf[:, t:t + 1], ALU.pow).then_inc(rstd3_ready, 1)


def constants():
    half = RET_QK // 2
    inv = (np.float32(10000.0) ** (-np.arange(half, dtype=np.float32) / np.float32(half))).astype(np.float32)
    ang = np.arange(S, dtype=np.float32)[:, None] * inv[None, :]
    cs = np.stack([np.cos(ang), np.sin(ang)]).astype(np.float32)
    rope = np.ascontiguousarray(cs.reshape(2, TILES, P, half).transpose(2, 0, 1, 3))
    n = np.arange(S)
    lg = np.log1p(-np.exp2(-5.0 - np.arange(RET_HEADS)))
    full = np.exp(lg[:, None, None] * np.abs(n[:, None] - n[None, :])) * RET_QK ** -0.5
    full = full * (n[:, None] // CHUNK <= n[None, :] // CHUNK)
    decay = np.concatenate([full[:, :P, :], full[:, P:, P:]], axis=2).transpose(1, 0, 2)
    return np.eye(P, dtype=np.float32), rope, np.ascontiguousarray(decay.astype(np.float32))


def kernel(x, norm_mix_g, w_in, ret_norm_g, attn_sinks, w_ret_branch, w_attn_branch, w_gate, w_out,
           norm_ffn_g, w_up, w_down, norm_final_g):
    import concourse.bacc as _bacc
    from concourse.bass_utils import run_bass_kernel_spmd as _run

    nc = _bacc.Bacc("TRN2", target_bir_lowering=False, num_devices=1)
    ident, rope, decay = constants()

    def columns(g):
        return np.asarray(g).reshape(KCH, P).T

    sinks = np.repeat(np.asarray(attn_sinks).reshape(16, 2).T, P // 2, axis=0)
    small = np.concatenate([ident, rope.reshape(P, -1), columns(norm_mix_g), columns(ret_norm_g),
                            columns(norm_ffn_g), sinks], axis=1)
    given = {
        "x": np.asarray(x)[0], "x_t": np.asarray(x)[0].reshape(S, KCH, P).transpose(2, 1, 0), "w_in": np.asarray(w_in)[0],
        "w_ret": np.asarray(w_ret_branch)[0], "w_att": np.asarray(w_attn_branch)[0],
        "w_gate": np.asarray(w_gate)[0], "w_out": np.asarray(w_out)[0],
        "w_up": np.asarray(w_up)[0], "w_down": np.asarray(w_down)[0],
        "g_fin": np.asarray(norm_final_g), "small_c": small, "decay_c": decay,
    }
    arrays, args = {}, {}
    for name, a in given.items():
        arrays["in_" + name] = np.ascontiguousarray(a)
        args[name] = nc.dram_tensor("in_" + name, a.shape, mybir.dt.float32, kind="ExternalInput").ap()
    out = nc.dram_tensor("out_0", (S, D), mybir.dt.float32, kind="ExternalOutput").ap()
    build(nc, out=out, **args)
    r = _run(nc, [arrays], core_ids=[0])
    return r.results[0]["out_0"].reshape(1, S, D)
```
